# Optimizing a Trainium2 kernel written in Bass

```python
import math
import jax, jax.numpy as jnp
from jax import lax
import numpy as np

D_MODEL = 1024
BATCH = 1
SEQ = 256
DEPTH = 2

HEAD_DIM = 64
MEM_HEADS = 4
MEM_WIDTH = MEM_HEADS * HEAD_DIM
SB_HEADS = (D_MODEL - MEM_WIDTH) // (2 * HEAD_DIM)
MOBA_HEADS = SB_HEADS
SB_WIDTH = SB_HEADS * HEAD_DIM
MOBA_WIDTH = MOBA_HEADS * HEAD_DIM
MIX_WIDTH = SB_WIDTH + MOBA_WIDTH + MEM_WIDTH
IN_COLS = 4 * SB_WIDTH + 4 * MOBA_WIDTH + 2 * MEM_WIDTH
MEM_LEN = 256
SB_BLOCK = 128
MOBA_BLOCK = 256
MOBA_TOPK = 3
MOBA_Q_CHUNK = 64
ROPE_THETA = 500000.0
ROPE_DIMS = HEAD_DIM // 4
NORM_EPS = 1e-6
NEG_INF = -1e30


def rms_norm(x, g):
    xf = x.astype(jnp.float32)
    y = xf * lax.rsqrt(jnp.mean(xf * xf, axis=-1, keepdims=True) + NORM_EPS)
    return (y * g.astype(jnp.float32)).astype(x.dtype)

def split_heads(t, n_heads):
    b, s, _ = t.shape
    return t.reshape(b, s, n_heads, HEAD_DIM).transpose(0, 2, 1, 3)

def merge_heads(t):
    b, h, s, d = t.shape
    return t.transpose(0, 2, 1, 3).reshape(b, s, h * d)

def partial_rotary(t, pos):
    half = ROPE_DIMS // 2
    inv_freq = jnp.float32(ROPE_THETA) ** (-jnp.arange(half, dtype=jnp.float32) * 2.0 / ROPE_DIMS)
    ang = pos.astype(jnp.float32)[:, None] * inv_freq[None, :]
    cos, sin = jnp.cos(ang), jnp.sin(ang)
    tf = t.astype(jnp.float32)
    x1, x2, rest = tf[..., :half], tf[..., half:ROPE_DIMS], tf[..., ROPE_DIMS:]
    out = jnp.concatenate([x1 * cos - x2 * sin, x2 * cos + x1 * sin, rest], axis=-1)
    return out.astype(t.dtype)

def stick_breaking_attention(q, k, v):
    T = q.shape[2]
    scale = HEAD_DIM ** -0.5
    outs = []
    for i in range(T // SB_BLOCK):
        q0, q1 = i * SB_BLOCK, (i + 1) * SB_BLOCK
        qb = q[:, :, q0:q1]
        kb, vb = k[:, :, :q1], v[:, :, :q1]
        z = jnp.einsum('bhqd,bhkd->bhqk', qb, kb, preferred_element_type=jnp.float32) * scale
        past = jnp.arange(q1)[None, :] < jnp.arange(q0, q1)[:, None]
        log_beta = jax.nn.log_sigmoid(z)
        log_one_minus = jnp.where(past, log_beta - z, 0.0)
        later = lax.cumsum(log_one_minus, axis=3, reverse=True) - log_one_minus
        w = jnp.where(past, jnp.exp(log_beta + later), 0.0)
        outs.append(jnp.einsum('bhqk,bhkd->bhqd', w.astype(v.dtype), vb))
    return jnp.concatenate(outs, axis=2)

def moba_attention(q, k, v):
    B, H, T, dh = q.shape
    n_blk = -(-T // MOBA_BLOCK)
    Tp = n_blk * MOBA_BLOCK
    pad = [(0, 0), (0, 0), (0, Tp - T), (0, 0)]
    kp, vp = jnp.pad(k, pad), jnp.pad(v, pad)
    kblk = kp.reshape(B, H, n_blk, MOBA_BLOCK, dh)
    vblk = vp.reshape(B, H, n_blk, MOBA_BLOCK, dh)
    kmean = jnp.mean(kblk.astype(jnp.float32), axis=3)
    topk = min(MOBA_TOPK, n_blk - 1)
    scale = dh ** -0.5
    bi = jnp.arange(B)[:, None, None, None]
    hi = jnp.arange(H)[None, :, None, None]

    def chunk(ci):
        c0 = ci * MOBA_Q_CHUNK
        qc = lax.dynamic_slice_in_dim(q, c0, MOBA_Q_CHUNK, axis=2)
        t_pos = c0 + jnp.arange(MOBA_Q_CHUNK)
        own = c0 // MOBA_BLOCK
        own_start = own * MOBA_BLOCK
        k_own = lax.dynamic_slice_in_dim(kp, own_start, MOBA_BLOCK, axis=2)
        v_own = lax.dynamic_slice_in_dim(vp, own_start, MOBA_BLOCK, axis=2)
        s_own = jnp.einsum('bhqd,bhkd->bhqk', qc, k_own, preferred_element_type=jnp.float32) * scale
        causal = (own_start + jnp.arange(MOBA_BLOCK))[None, :] <= t_pos[:, None]
        s_own = jnp.where(causal, s_own, NEG_INF)
        if topk > 0:
            gate = jnp.einsum('bhqd,bhnd->bhqn', qc.astype(jnp.float32), kmean)
            gate = jnp.where(jnp.arange(n_blk) < own, gate, -jnp.inf)
            _, sel = lax.top_k(gate, topk)
            sel_valid = sel < own
            k_sel = kblk[bi, hi, sel]
            v_sel = vblk[bi, hi, sel]
            s_sel = jnp.einsum('bhqd,bhqnkd->bhqnk', qc, k_sel, preferred_element_type=jnp.float32) * scale
            s_sel = jnp.where(sel_valid[..., None], s_sel, NEG_INF)
            s_sel = s_sel.reshape(B, H, MOBA_Q_CHUNK, topk * MOBA_BLOCK)
            p = jax.nn.softmax(jnp.concatenate([s_sel, s_own], axis=-1), axis=-1)
            p_sel = p[..., :topk * MOBA_BLOCK].reshape(B, H, MOBA_Q_CHUNK, topk, MOBA_BLOCK)
            p_own = p[..., topk * MOBA_BLOCK:]
            o = (jnp.einsum('bhqnk,bhqnkd->bhqd', p_sel.astype(v.dtype), v_sel)
                 + jnp.einsum('bhqk,bhkd->bhqd', p_own.astype(v.dtype), v_own))
        else:
            p_own = jax.nn.softmax(s_own, axis=-1)
            o = jnp.einsum('bhqk,bhkd->bhqd', p_own.astype(v.dtype), v_own)
        return o

    outs = lax.map(chunk, jnp.arange(T // MOBA_Q_CHUNK))
    return outs.transpose(1, 2, 0, 3, 4).reshape(B, H, T, dh)

def memory_attention(q, mk, mv):
    s = jnp.einsum('bhqd,bhmd->bhqm', q, mk, preferred_element_type=jnp.float32) * (HEAD_DIM ** -0.5)
    p = jax.nn.softmax(s, axis=-1)
    return jnp.einsum('bhqm,bhmd->bhqd', p.astype(mv.dtype), mv)

def first_inputs(seed: int = 0) -> dict:
    key = jax.random.key(seed)
    ks = jax.random.split(key, 8)
    x = jax.random.normal(ks[0], (BATCH, SEQ, D_MODEL), jnp.float32)
    mem = jax.random.normal(ks[1], (BATCH, MEM_LEN, D_MODEL), jnp.float32)
    norm_g = 1.0 + 0.02 * jax.random.normal(ks[2], (DEPTH, D_MODEL), jnp.float32)
    w_in = jax.random.normal(ks[3], (DEPTH, D_MODEL, IN_COLS), jnp.float32) * D_MODEL ** -0.5
    mem_norm_g = 1.0 + 0.02 * jax.random.normal(ks[4], (DEPTH, D_MODEL), jnp.float32)
    w_mem_kv = jax.random.normal(ks[5], (DEPTH, D_MODEL, 2 * MEM_WIDTH), jnp.float32) * D_MODEL ** -0.5
    w_out = jax.random.normal(ks[6], (DEPTH, MIX_WIDTH, D_MODEL), jnp.float32) * MIX_WIDTH ** -0.5
    final_norm_g = 1.0 + 0.02 * jax.random.normal(ks[7], (D_MODEL,), jnp.float32)
    return {"x": x, "mem": mem, "norm_g": norm_g, "w_in": w_in, "mem_norm_g": mem_norm_g,
            "w_mem_kv": w_mem_kv, "w_out": w_out, "final_norm_g": final_norm_g}

def first_block(x, mem, norm_g, w_in, mem_norm_g, w_mem_kv, w_out, final_norm_g):
    T = x.shape[1]
    pos = jnp.arange(T)
    widths = [SB_WIDTH] * 4 + [MOBA_WIDTH] * 4 + [MEM_WIDTH] * 2
    split_at = np.cumsum(widths)[:-1].tolist()
    for layer in range(DEPTH):
        h = rms_norm(x, norm_g[layer])
        proj = jnp.einsum('btd,dc->btc', h, w_in[layer])
        sb_q, sb_k, sb_v, sb_g, mb_q, mb_k, mb_v, mb_g, mem_q, mem_g = jnp.split(proj, split_at, axis=-1)

        o_sb = stick_breaking_attention(split_heads(sb_q, SB_HEADS), split_heads(sb_k, SB_HEADS),
                                        split_heads(sb_v, SB_HEADS))
        o_sb = merge_heads(o_sb) * jax.nn.silu(sb_g)

        q_mb = partial_rotary(split_heads(mb_q, MOBA_HEADS), pos)
        k_mb = partial_rotary(split_heads(mb_k, MOBA_HEADS), pos)
        o_mb = moba_attention(q_mb, k_mb, split_heads(mb_v, MOBA_HEADS))
        o_mb = merge_heads(o_mb) * jax.nn.silu(mb_g)

        m = rms_norm(mem, mem_norm_g[layer])
        mkv = jnp.einsum('bmd,dc->bmc', m, w_mem_kv[layer])
        mk, mv = jnp.split(mkv, 2, axis=-1)
        o_mem = memory_attention(split_heads(mem_q, MEM_HEADS), split_heads(mk, MEM_HEADS),
                                 split_heads(mv, MEM_HEADS))
        o_mem = merge_heads(o_mem) * jax.nn.silu(mem_g)

        mixed = jnp.concatenate([o_sb, o_mb, o_mem], axis=-1)
        x = x + jnp.einsum('btc,cd->btd', mixed, w_out[layer])
    return rms_norm(x, final_norm_g)


DEPTH_2 = 1

BLOCK = 128
N_META = 16
META_PAD = BLOCK - N_META
WINDOW = 128
ROPE_THETA_2 = 10000.0
RMS_EPS = 1e-6
NEG_INF_2 = -1e30

SWA_Q_HEADS = 16
SWA_KV_HEADS = 4
SWA_GROUP = SWA_Q_HEADS // SWA_KV_HEADS
SWA_WIDTH = SWA_Q_HEADS * HEAD_DIM

DIFF_HEADS = 8
DIFF_V_DIM = 2 * HEAD_DIM
DIFF_WIDTH = DIFF_HEADS * DIFF_V_DIM

D_FF = ((8 * D_MODEL // 3 + 255) // 256) * 256

QA_COLS = SWA_Q_HEADS * HEAD_DIM
KA_COLS = SWA_KV_HEADS * HEAD_DIM
VA_COLS = SWA_KV_HEADS * HEAD_DIM
QB_COLS = DIFF_HEADS * 2 * HEAD_DIM
KB_COLS = DIFF_HEADS * 2 * HEAD_DIM
VB_COLS = DIFF_WIDTH
GATE_COLS = 2 * D_MODEL
IN_COLS_2 = QA_COLS + KA_COLS + VA_COLS + QB_COLS + KB_COLS + VB_COLS + GATE_COLS
SPLITS = (
    QA_COLS,
    QA_COLS + KA_COLS,
    QA_COLS + KA_COLS + VA_COLS,
    QA_COLS + KA_COLS + VA_COLS + QB_COLS,
    QA_COLS + KA_COLS + VA_COLS + QB_COLS + KB_COLS,
    QA_COLS + KA_COLS + VA_COLS + QB_COLS + KB_COLS + VB_COLS,
)


def rms_norm_2(x, g):
    xf = x.astype(jnp.float32)
    y = xf * lax.rsqrt(jnp.mean(xf * xf, axis=-1, keepdims=True) + RMS_EPS)
    return (y * g.astype(jnp.float32)).astype(x.dtype)

def rope(x, pos):
    d = x.shape[-1]
    half = d // 2
    inv_freq = ROPE_THETA_2 ** (-jnp.arange(0, d, 2, dtype=jnp.float32) / d)
    ang = pos.astype(jnp.float32)[:, None] * inv_freq[None, :]
    shape = (1, x.shape[1]) + (1,) * (x.ndim - 3) + (half,)
    cos = jnp.cos(ang).reshape(shape)
    sin = jnp.sin(ang).reshape(shape)
    xf = x.astype(jnp.float32)
    x1, x2 = xf[..., :half], xf[..., half:]
    return jnp.concatenate([x1 * cos - x2 * sin, x2 * cos + x1 * sin], axis=-1).astype(x.dtype)

def windowed_gqa_sink_attention(q, k, v, sink, pos, is_real):
    B, Lp = q.shape[0], q.shape[1]
    nb = Lp // BLOCK
    scale = HEAD_DIM ** -0.5
    k_meta = k[:, META_PAD:BLOCK]
    v_meta = v[:, META_PAD:BLOCK]
    padw = ((0, 0), (BLOCK, BLOCK), (0, 0), (0, 0))
    k_p = jnp.pad(k, padw)
    v_p = jnp.pad(v, padw)
    pos_p = jnp.pad(pos, (BLOCK, BLOCK))
    real_p = jnp.pad(is_real, (BLOCK, BLOCK))
    qb = q.reshape(B, nb, BLOCK, SWA_KV_HEADS, SWA_GROUP, HEAD_DIM).transpose(1, 0, 2, 3, 4, 5)
    sink_g = sink.astype(jnp.float32).reshape(SWA_KV_HEADS, SWA_GROUP)

    def one_block(args):
        i, qi = args
        start = i * BLOCK
        kb = lax.dynamic_slice_in_dim(k_p, start, 3 * BLOCK, axis=1)
        vb = lax.dynamic_slice_in_dim(v_p, start, 3 * BLOCK, axis=1)
        kpos = lax.dynamic_slice_in_dim(pos_p, start, 3 * BLOCK)
        kreal = lax.dynamic_slice_in_dim(real_p, start, 3 * BLOCK)
        qpos = lax.dynamic_slice_in_dim(pos, start, BLOCK)
        mask = kreal[None, :] & (jnp.abs(qpos[:, None] - kpos[None, :]) <= WINDOW)
        s_band = jnp.einsum('bqhgd,bkhd->bhgqk', qi, kb).astype(jnp.float32) * scale
        s_band = jnp.where(mask, s_band, NEG_INF_2)
        s_meta = jnp.einsum('bqhgd,bmhd->bhgqm', qi, k_meta).astype(jnp.float32) * scale
        s_sink = jnp.broadcast_to(sink_g[None, :, :, None, None], s_meta.shape[:-1] + (1,))
        p = jax.nn.softmax(jnp.concatenate([s_band, s_meta, s_sink], axis=-1), axis=-1)
        p_band = p[..., :3 * BLOCK].astype(v.dtype)
        p_meta = p[..., 3 * BLOCK:3 * BLOCK + N_META].astype(v.dtype)
        return (jnp.einsum('bhgqk,bkhd->bqhgd', p_band, vb)
                + jnp.einsum('bhgqm,bmhd->bqhgd', p_meta, v_meta))

    o = lax.map(one_block, (jnp.arange(nb), qb))
    return o.transpose(1, 0, 2, 3, 4, 5).reshape(B, Lp, SWA_WIDTH)

def differential_attention(q, k, v, lam, lambda_init, subln_gain, is_key):
    B, Lp = q.shape[0], q.shape[1]
    nb = Lp // BLOCK
    scale = HEAD_DIM ** -0.5
    key_bias = jnp.where(is_key, 0.0, NEG_INF_2).astype(jnp.float32)
    qb = q.reshape(B, nb, BLOCK, DIFF_HEADS, 2, HEAD_DIM).transpose(1, 0, 2, 3, 4, 5)

    def one_block(qi):
        s = jnp.einsum('bqhcd,bkhcd->bhcqk', qi, k).astype(jnp.float32) * scale + key_bias
        p = jax.nn.softmax(s, axis=-1)
        a = (p[:, :, 0] - lam * p[:, :, 1]).astype(v.dtype)
        return jnp.einsum('bhqk,bkhe->bqhe', a, v)

    o = lax.map(one_block, qb)
    o = o.transpose(1, 0, 2, 3, 4).reshape(B, Lp, DIFF_HEADS, DIFF_V_DIM)
    o = rms_norm_2(o, subln_gain) * (1.0 - lambda_init)
    return o.reshape(B, Lp, DIFF_WIDTH).astype(v.dtype)

def second_inputs(seed: int = 0) -> dict:
    key = jax.random.key(seed)
    ks = jax.random.split(key, 20)
    f32 = jnp.float32

    def nrm(k, shape, scale):
        return jax.random.normal(k, shape, f32) * scale

    def gain(k, shape):
        return 1.0 + 0.02 * jax.random.normal(k, shape, f32)

    return {
        "x": nrm(ks[0], (BATCH, SEQ, D_MODEL), 1.0),
        "meta_tokens": nrm(ks[1], (N_META, D_MODEL), 1.0),
        "pre_mix_gain": gain(ks[2], (DEPTH_2, D_MODEL)),
        "w_in": nrm(ks[3], (DEPTH_2, D_MODEL, IN_COLS_2), D_MODEL ** -0.5),
        "b_gate": nrm(ks[4], (DEPTH_2, GATE_COLS), 0.1),
        "attn_sink": nrm(ks[5], (DEPTH_2, SWA_Q_HEADS), 0.5),
        "lambda_q1": nrm(ks[6], (DEPTH_2, HEAD_DIM), 0.1),
        "lambda_k1": nrm(ks[7], (DEPTH_2, HEAD_DIM), 0.1),
        "lambda_q2": nrm(ks[8], (DEPTH_2, HEAD_DIM), 0.1),
        "lambda_k2": nrm(ks[9], (DEPTH_2, HEAD_DIM), 0.1),
        "diff_subln_gain": gain(ks[10], (DEPTH_2, DIFF_V_DIM)),
        "w_branch_swa": nrm(ks[11], (DEPTH_2, SWA_WIDTH, D_MODEL), SWA_WIDTH ** -0.5),
        "w_branch_diff": nrm(ks[12], (DEPTH_2, DIFF_WIDTH, D_MODEL), DIFF_WIDTH ** -0.5),
        "w_out": nrm(ks[13], (DEPTH_2, D_MODEL, D_MODEL), D_MODEL ** -0.5),
        "post_mix_gain": gain(ks[14], (DEPTH_2, D_MODEL)),
        "pre_ffn_gain": gain(ks[15], (DEPTH_2, D_MODEL)),
        "w_ffn_in": nrm(ks[16], (DEPTH_2, D_MODEL, 2 * D_FF), D_MODEL ** -0.5),
        "w_ffn_out": nrm(ks[17], (DEPTH_2, D_FF, D_MODEL), D_FF ** -0.5),
        "post_ffn_gain": gain(ks[18], (DEPTH_2, D_MODEL)),
    }

def second_block(x, meta_tokens, pre_mix_gain, w_in, b_gate, attn_sink, lambda_q1, lambda_k1,
              lambda_q2, lambda_k2, diff_subln_gain, w_branch_swa, w_branch_diff, w_out,
              post_mix_gain, pre_ffn_gain, w_ffn_in, w_ffn_out, post_ffn_gain):
    B = x.shape[0]
    filler = jnp.zeros((B, META_PAD, D_MODEL), x.dtype)
    meta = jnp.broadcast_to(meta_tokens[None].astype(x.dtype), (B, N_META, D_MODEL))
    h = jnp.concatenate([filler, meta, x], axis=1)
    Lp = h.shape[1]
    pos = jnp.arange(Lp, dtype=jnp.int32) - META_PAD
    is_real = pos >= N_META
    is_key = pos >= 0

    for l in range(DEPTH_2):
        lambda_init = 0.8 - 0.6 * math.exp(-0.3 * l)
        u = rms_norm_2(h, pre_mix_gain[l])
        proj = u @ w_in[l]
        qa, ka, va, qb, kb, vb, g = jnp.split(proj, SPLITS, axis=-1)
        qa = rope(qa.reshape(B, Lp, SWA_Q_HEADS, HEAD_DIM), pos)
        ka = rope(ka.reshape(B, Lp, SWA_KV_HEADS, HEAD_DIM), pos)
        va = va.reshape(B, Lp, SWA_KV_HEADS, HEAD_DIM)
        qb = rope(qb.reshape(B, Lp, DIFF_HEADS, 2, HEAD_DIM), pos)
        kb = rope(kb.reshape(B, Lp, DIFF_HEADS, 2, HEAD_DIM), pos)
        vb = vb.reshape(B, Lp, DIFF_HEADS, DIFF_V_DIM)

        o_swa = windowed_gqa_sink_attention(qa, ka, va, attn_sink[l], pos, is_real)
        lam = (jnp.exp(jnp.sum(lambda_q1[l].astype(jnp.float32) * lambda_k1[l].astype(jnp.float32)))
               - jnp.exp(jnp.sum(lambda_q2[l].astype(jnp.float32) * lambda_k2[l].astype(jnp.float32)))
               + lambda_init)
        o_diff = differential_attention(qb, kb, vb, lam, lambda_init, diff_subln_gain[l], is_key)

        gates = jax.nn.sigmoid(g + b_gate[l])
        g_swa, g_diff = gates[..., :D_MODEL], gates[..., D_MODEL:]
        merged = g_swa * (o_swa @ w_branch_swa[l]) + g_diff * (o_diff @ w_branch_diff[l])
        h = h + rms_norm_2(merged @ w_out[l], post_mix_gain[l])

        u = rms_norm_2(h, pre_ffn_gain[l])
        gate_up = u @ w_ffn_in[l]
        f = (jax.nn.silu(gate_up[..., :D_FF]) * gate_up[..., D_FF:]) @ w_ffn_out[l]
        h = h + rms_norm_2(f, post_ffn_gain[l])

    return h[:, BLOCK:]


def setup_inputs(seed=0):
    out = dict(first_inputs(seed))
    for name, value in second_inputs(seed + 1).items():
        if name != "x":
            out[name + "_2"] = value
    return out


def reference(
    x, mem, norm_g, w_in, mem_norm_g, w_mem_kv, w_out, final_norm_g, meta_tokens_2,
    pre_mix_gain_2, w_in_2, b_gate_2, attn_sink_2, lambda_q1_2, lambda_k1_2, lambda_q2_2,
    lambda_k2_2, diff_subln_gain_2, w_branch_swa_2, w_branch_diff_2, w_out_2, post_mix_gain_2,
    pre_ffn_gain_2, w_ffn_in_2, w_ffn_out_2, post_ffn_gain_2,
):
    x = first_block(
        x, mem, norm_g, w_in, mem_norm_g, w_mem_kv, w_out, final_norm_g,
    )
    return second_block(
        x, meta_tokens_2, pre_mix_gain_2, w_in_2, b_gate_2, attn_sink_2, lambda_q1_2,
        lambda_k1_2, lambda_q2_2, lambda_k2_2, diff_subln_gain_2, w_branch_swa_2,
        w_branch_diff_2, w_out_2, post_mix_gain_2, pre_ffn_gain_2, w_ffn_in_2, w_ffn_out_2,
        post_ffn_gain_2,
    )


_drawn_inputs = setup_inputs


def setup_inputs(seed=0):
    import zlib

    import numpy as np

    out = dict(_drawn_inputs(seed))
    spreads = {}
    factors = {'norm_g': 3.161,
     'mem_norm_g': 8.0,
     'attn_sink_2': 64.0,
     'diff_subln_gain_2': 3.383,
     'post_mix_gain_2': 3.394,
     'pre_ffn_gain_2': 3.45,
     'post_ffn_gain_2': 16.605}
    for name, (base, spread) in spreads.items():
        noise = np.random.default_rng([zlib.crc32(name.encode()), seed]).standard_normal(out[name].shape)
        drawn = base * np.exp(spread * noise) if base else spread * noise
        out[name] = __import__('jax').numpy.asarray(drawn.astype(out[name].dtype))
    for name, factor in factors.items():
        out[name] = (out[name] * factor).astype(out[name].dtype)
    return out
```

```python
import math
from contextlib import ExitStack

import numpy as np

import concourse.bass as bass
from concourse import mybir

F32 = mybir.dt.float32
F32R = mybir.dt.float32r
BF16 = mybir.dt.bfloat16
ACT = mybir.ActivationFunctionType
ALU = mybir.AluOpType
AX = mybir.AxisListType

P = 128
D = 1024
T = 256
NT = T // P
KC = D // P
DEPTH = 2
DH = 64
MEM_HEADS = 4
MEMW = MEM_HEADS * DH
SBW = (D - MEMW) // 2
IN1 = 8 * SBW + 2 * MEMW
ROPE1 = DH // 4
THETA1, THETA2 = 500000.0, 10000.0
EPS = 1e-6
NEG = -1e30
META = 16
KVH = 4
QA, KA, VA = 1024, 256, 256
QB = KB = VB = 1024
IN2 = QA + KA + VA + QB + KB + VB + 2 * D
DIFF_HEADS = 8
DFF = ((8 * D // 3 + 255) // 256) * 256
LAMBDA_INIT = 0.8 - 0.6 * math.exp(-0.3 * 0)
SCALE = DH ** -0.5

NSLOT = 5
UK = 2
NSTAGE = 3
NGAIN = 2
SMALL = 7
SPLIT_AHEAD = 3

C_ID, C_TRI, C_ONE = 0, 128, 256
C_COS1 = 384
C_SIN1 = C_COS1 + NT * ROPE1
C_COS2 = C_SIN1 + NT * ROPE1
C_SIN2 = C_COS2 + NT * DH
C_COSM = C_SIN2 + NT * DH
C_SINM = C_COSM + DH
C_END = C_SINM + DH
B_ID, B_SB, B_LOW, B_UP, B_END = 0, 128, 256, 384, 512


def constant_tables():
    f = np.zeros((P, C_END), np.float32)
    j = np.arange(P)
    f[:, C_ID:C_ID + P] = np.eye(P)
    f[:, C_TRI:C_TRI + P] = -(j[:, None] >= j[None, :]).astype(np.float32)
    f[:, C_ONE:C_ONE + P] = -1.0

    def angles(pos, theta, dims):
        inv = np.float32(theta) ** (-np.arange(dims // 2, dtype=np.float32) * np.float32(2.0) / np.float32(dims))
        a = pos.astype(np.float32)[:, None] * inv.astype(np.float32)[None, :]
        c, s = np.cos(a.astype(np.float64)), np.sin(a.astype(np.float64))
        return np.concatenate([c, c], 1), np.concatenate([-s, s], 1)

    for t in range(NT):
        c, s = angles(t * P + j, THETA1, ROPE1)
        f[:, C_COS1 + t * ROPE1:C_COS1 + (t + 1) * ROPE1] = c
        f[:, C_SIN1 + t * ROPE1:C_SIN1 + (t + 1) * ROPE1] = s
        c, s = angles(META + t * P + j, THETA2, DH)
        f[:, C_COS2 + t * DH:C_COS2 + (t + 1) * DH] = c
        f[:, C_SIN2 + t * DH:C_SIN2 + (t + 1) * DH] = s
    c, s = angles(np.arange(META), THETA2, DH)
    f[:META, C_COSM:C_COSM + DH] = c
    f[:META, C_SINM:C_SINM + DH] = s
    b = np.zeros((P, B_END), np.float32)
    b[:, B_ID:B_ID + P] = np.eye(P)
    r, c = j[:, None], j[None, :]
    b[:, B_SB:B_SB + P] = np.where(r < c, 0.0, NEG)
    b[:, B_LOW:B_LOW + P] = np.where(c <= r, 0.0, NEG)
    b[:, B_UP:B_UP + P] = np.where(r <= c, 0.0, NEG)
    return f, b


KINDS = {
    "sb": dict(n=512, q=0, k=128, v=256, g=384, heads=2, qw=128),
    "mb": dict(n=512, q=0, k=128, v=256, g=384, heads=2, qw=128),
    "mem": dict(n=512, q=0, g=128, k=256, v=384, heads=2, qw=128),
    "swa": dict(n=384, q=0, k=256, v=384, heads=4, qw=256),
    "diff": dict(n=384, q=0, k=128, v=256, heads=1, qw=128),
}


class Plan:

    def __init__(self):
        self.groups, self.steps, self.units = [], [], []
        self.bank_user = {}
        self.count = dict.fromkeys(("attn", "evac_act", "evac_dve", "jobs", "softs", "sbs", "outs", "batches",
                                    "halves", "gated", "roped", "pts", "blends", "norms", "rstd", "norm_done",
                                    "groups"), 0)

    def next(self, name, n=1):
        self.count[name] += n
        return self.count[name]

    def group(self, kind, banks, units, **kw):
        g = dict(kind=kind, banks=banks, gi=len(self.groups), **kw)
        if kind in KINDS:
            g["ga"] = self.next("attn") - 1
            g["by"] = "evac_act"
        else:
            g["by"] = None if kind in ("wo2", "fout") else "evac_dve"
        g["prev"] = [self.bank_user.get(b) for b in banks]
        for t, b in enumerate(banks):
            self.bank_user[b] = (g, t)
        g["units"] = [dict(loads=loads, parts=parts, chunks=chunks, g=g, first=(n == 0), last=(n == len(units) - 1))
                      for n, (chunks, loads, parts) in enumerate(units)]
        self.groups.append(g)
        return g


def attention_slots(g):
    kind = g["kind"]
    K = KINDS[kind]
    heads = K["heads"]
    slots = {n: [] for n in range(12)}
    slots[0].append(("evac", dict(g=g)))
    if kind in ("mb", "swa", "diff"):
        slots[0].append(("rope", dict(g=g)))
    if "g" in K:
        slots[0].append(("gate", dict(g=g)))
    jobs = [dict(g=g, a=a) for a in range(2 if kind == "diff" else heads)]
    if kind == "sb":
        slots[1].append(("turn_qk", dict(g=g, part=0)))
        for a, j in enumerate(jobs):
            slots[6 + a].append(("out", j))
        for a, j in enumerate(jobs):
            slots[2 + a].append(("scores", j))
            slots[4 + a].append(("later", j))
        slots[8].append(("turn_mix", dict(g=g)))
    elif kind == "diff":
        slots[2].append(("turn_qk", dict(g=g, part=0)))
        slots[3].append(("turn_qk", dict(g=g, part=1)))
        for a, j in enumerate(jobs):
            slots[4 + a].append(("scores", j))
        slots[6].append(("blend", jobs[0]))
        slots[7].append(("turn_p", jobs[0]))
        slots[8].append(("out", jobs[0]))
        slots[10].append(("turn_mix", dict(g=g)))
    else:
        wide = kind == "swa"
        if wide:
            slots[2].append(("turn_qk", dict(g=g, part=0)))
            slots[3].append(("turn_qk", dict(g=g, part=1)))
        else:
            slots[1].append(("turn_qk", dict(g=g, part=0)))
        at = 4 if wide else 2
        for a, j in enumerate(jobs):
            slots[at + 2 + a].append(("turn_p", j))
        for a, j in enumerate(jobs):
            slots[at + 3 + a].append(("out", j))
        for a, j in enumerate(jobs):
            slots[at + a].append(("scores", j))
        slots[at + 3 + heads].append(("turn_mix", dict(g=g)))
    return slots


def lay_out(timeline):
    due, steps, at = {}, [], 0
    for what, arg in timeline:
        if what == "unit":
            steps.append(("unit", arg))
            g = arg["g"]
            if arg["last"]:
                if g["kind"] in KINDS:
                    for n, some in attention_slots(g).items():
                        due.setdefault(at + n, []).extend(some)
                elif g["by"]:
                    steps.append(("evac", dict(g=g)))
            steps.extend(due.pop(at, []))
            at += 1
        elif what == "flush":
            for k in sorted(due):
                steps.extend(due[k])
            due = {}
        else:
            steps.append((what, arg))
    assert not due
    return steps


def number(pl, steps):
    slot_dmas = [0] * NSLOT
    reader = {}
    probs_reader = {}
    outs_of_pt = []
    meta_turned = {}
    x_ready = [("s_x", 16)] * NT
    xn_ready = {}
    mem_ready = [("s_small", 16 * SMALL)] * NT
    before = None
    for what, s in steps:
        g = s.get("g") if isinstance(s, dict) else None
        if what == "unit":
            u = len(pl.units)
            s["u"], s["slot"] = u, u % NSLOT
            slot_dmas[s["slot"]] += 16 * sum(1 if load[1] == 1 else UK for load in s["loads"])
            s["landed"] = slot_dmas[s["slot"]]
            s["width"] = sum(reps * width for _, reps, _, _, _, _, width in s["loads"])
            pl.units.append(s)
            for name, *_ in s["parts"]:
                for c in range(*s["chunks"]):
                    reader[("m", c % KC) if name == "f" else (name, c)] = u
            if s["last"]:
                g["t_done"] = [("group_done", pl.next("groups")), ("unit_used", u + 1)]
        elif what == "evac":
            g["free"] = [pl.next(g["by"]) for _ in range(NT)]
            if g["kind"] == "wo":
                x_ready = [("evac_dve", f) for f in g["free"]]
            elif g["kind"] == "bdiff":
                xn_ready[g["n"]] = [("evac_dve", f) for f in g["free"]]
        elif what == "rope":
            g["roped"] = pl.next("roped")
        elif what == "gate":
            s["n"] = pl.next("gated") - 1
        elif what == "scores":
            s["j"] = j = pl.next("jobs") - 1
            s["p_free"] = probs_reader.get(j % 4)
            s["meta_out"] = meta_turned.get(j % 2)
            if g["kind"] == "sb":
                s["sb"] = pl.next("sbs") - 1
            else:
                s["soft"] = pl.next("softs") - 1
            g["last_scores"] = j + 1
        elif what == "turn_qk":
            s["batch"] = pl.next("batches") - 1
            g["qk_ready"] = s["batch"] + 1
        elif what == "blend":
            s["blended"] = pl.next("blends")
            probs_reader[(s["j"] + 1) % 4] = ("blended", s["blended"])
        elif what == "turn_p":
            s["batch"] = pl.next("batches") - 1
            s["pt"] = pl.next("pts") - 1
            s["pt_free"] = outs_of_pt[s["pt"] - 2] if s["pt"] >= 2 else None
            probs_reader[s["j"] % 4] = ("tp_done", s["batch"] + 1)
            if g["kind"] in ("swa", "diff"):
                meta_turned[s["j"] % 2] = s["batch"] + 1
        elif what == "out":
            s["o"] = pl.next("outs") - 1
            s["first_out"] = "last_out" not in g
            g["last_out"] = s["o"] + 1
            if g["kind"] == "sb":
                probs_reader[s["j"] % 4] = ("out_done", s["o"] + 1)
            else:
                outs_of_pt.append(s["o"] + 1)
        elif what in ("norm", "addnorm", "metanorm"):
            s["n"] = pl.next("norms") - 1
            if what == "metanorm":
                s["ready"] = [("s_meta", 16)]
            elif what == "addnorm":
                s["ready"] = [("unit_used", len(pl.units))] * NT
            else:
                s["ready"] = mem_ready if s["source"] == "mem" else x_ready
            s["rstd"] = [pl.next("rstd") for _ in s["ready"]]
            s["done"] = [pl.next("norm_done") for _ in s["ready"]]
            done = [("norm_done", n) for n in s["done"]]
            if what == "addnorm" or s["dest"] == "x":
                x_ready = done
            elif s["dest"] == "xn":
                xn_ready = {0: done, 1: done}
            else:
                other_ready = done
        if what.startswith("turn_") and what not in ("turn_qk", "turn_p"):
            s["batch"] = pl.next("batches") - 1
            s["half"] = pl.next("halves")
            if what == "turn_norm":
                s["ready"] = (xn_ready[s["c"] // 4] if s["source"] == "xn" else other_ready)[s["t"]]
                places = [(s["dest"], s["c"] + k) for k in range(4)]
            elif what == "turn_meta":
                s["ready"] = other_ready[0]
                places = [("h", s["c"] + k) for k in range(4)]
            elif what == "turn_f":
                places = [("m", (2 * s["j"] + c) % KC) for c in range(2)]
            else:
                places = g["mix"]
                g["mixed"] = s["batch"] + 1
            last = [reader[p] + 1 for p in places if p in reader]
            s["dest_free"] = ("unit_used", max(last)) if last else None
            s["alone"] = before not in ("turn_norm", "turn_meta", "turn_f")
            s["outs_before"] = pl.count["outs"]
        if what.startswith("turn_"):
            before = what


def make_plan(W):
    pl = Plan()
    line = []

    def cols(w, rows, *ranges):
        return (w, rows, ranges)

    def add(gi):
        line.extend(("unit", u) for u in gi["units"])

    def units_of(loads_of, parts, chunks=KC):
        return [((c, c + UK), loads_of(c), parts) for c in range(0, chunks, UK)]

    def norm_turns(source, dest, off=0):
        for t in range(NT):
            for c in range(0, KC, 4):
                line.append(("turn_norm", dict(source=source, dest=dest, t=t, c=c, off=off)))

    w1 = [W["w_in"][layer] for layer in range(DEPTH)]
    h = 0
    for layer in range(DEPTH):
        line.append(("norm", dict(source="x", dest="xn", gain=True)))
        norm_turns("xn", "h", META)
        line.append(("norm", dict(source="mem", dest="mem_n", gain=True)))
        norm_turns("mem_n", "m")
        for kind, count in (("sb", 3), ("mb", 3), ("mem", 2)):
            for p in range(count):
                base = {"sb": 0, "mb": 4 * SBW, "mem": 8 * SBW}[kind]
                if kind != "mem":
                    def loads(c, base=base, p=p):
                        return [(0, 4, w1[layer], c, base + p * P, SBW, P)]
                    parts = [("h", 0, 512, 0)]
                else:
                    def loads(c, base=base, p=p):
                        return [(0, 2, w1[layer], c, base + p * P, MEMW, P),
                                (256, 2, W["w_mem_kv"][layer], c, p * P, MEMW, P)]
                    parts = [("h", 0, 256, 0), ("m", 256, 512, 256)]
                gi = pl.group(kind, (0, 1) if h % 2 == 0 else (2, 3), units_of(loads, parts), layer=layer,
                              pair=p, mix=[("mix", {"sb": 0, "mb": 3, "mem": 6}[kind] + p)])
                h += 1
                add(gi)
        outs = []
        for n in range(2):
            def loads(c, n=n):
                return [(0, 1, W["w_out"][layer], c, n * 512, 0, 512)]
            outs.append(pl.group("wo", (0, 1) if h % 2 == 0 else (2, 3),
                                 units_of(loads, [("mix", 0, 512, 0)]), layer=layer, n=n))
            h += 1
        a, b = (o["units"] for o in outs)
        order = a[:3] + b[:3]
        line.extend(("unit", u) for u in order)
        line.append(("flush", None))
        line.extend(("unit", u) for u in (a[3], b[3]))
    w2 = W["w_in_2"]
    line.append(("norm", dict(source="x", dest="x", gain=True)))
    line.append(("norm", dict(source="x", dest="xn", gain=True)))
    norm_turns("xn", "h", META)
    line.append(("metanorm", dict(dest="meta_n")))
    for c in (0, 4):
        line.append(("turn_meta", dict(c=c)))
    line.append(("gates_in", None))
    for n in range(4):
        def loads(c, n=n):
            return [(0, 1, w2, c, IN2 - 2 * D + n * 512, 0, 512)]
        add(pl.group("gates", (0, 1) if n % 2 == 0 else (2, 3), units_of(loads, [("h", 0, 512, 0)]), n=n))
    line.append(("gates_out", None))
    for kv in range(KVH):
        def loads(c, kv=kv):
            return [(0, 1, w2, c, kv * 256, 0, 256), (256, 2, w2, c, QA + kv * DH, KA, DH)]
        add(pl.group("swa", (0, 1), units_of(loads, [("h", 0, 384, 0)]), kv=kv, meta=[(256, 384, 0, 384)],
                     mix=[("mix", 2 * kv), ("mix", 2 * kv + 1)]))
    for d in range(DIFF_HEADS):
        def loads(c, d=d):
            return [(0, 3, w2, c, QA + KA + VA + d * P, QB, P)]
        add(pl.group("diff", (0, 1), units_of(loads, [("h", 0, 384, 0)]), d=d,
                     meta=[(128, 256, 0, 384), (256, 384, 1, 384)], mix=[("m", d)]))
    for n in range(2):
        def loads(c, n=n):
            return [(0, 1, W["w_branch_swa_2"], c, n * 512, 0, 512)]
        add(pl.group("bswa", (0, 1), units_of(loads, [("mix", 0, 512, 0)]), n=n))
    line.append(("flush", None))
    line.append(("settle", None))
    for n in range(2):
        def loads(c, n=n):
            return [(0, 1, W["w_branch_diff_2"], c, n * 512, 0, 512)]
        add(pl.group("bdiff", (2, 3) if n == 0 else (4, 5), units_of(loads, [("m", 0, 512, 0)]), n=n))
    norm_turns("xn", "mix")
    for n in range(2):
        def loads(c, n=n):
            return [(0, 1, W["w_out_2"], c, n * 512, 0, 512)]
        add(pl.group("wo2", (n, 2 + n), units_of(loads, [("mix", 0, 512, 0)]), n=n))
    line.append(("addnorm", dict(final=False)))
    line.append(("norm", dict(source="x", dest="xn", gain=True)))
    norm_turns("xn", "h", META)
    line.append(("silu_in", None))
    nf = DFF // 256
    fin = []
    for j in range(nf):
        def loads(c, j=j):
            return [(0, 2, W["w_ffn_in_2"], c, j * 256, DFF, 256)]
        fin.append((j, units_of(loads, [("h", 0, 512, 0)])))

    fo = [pl.group("fout", (n, 2 + n), [], n=n) for n in range(2)]

    def add_out(j):
        for n in range(2):
            line.append(("unit", dict(loads=[(0, 1, W["w_ffn_out_2"], 2 * j, n * 512, 0, 512)],
                                      parts=[("f", 0, 512, 0)], chunks=(2 * j, 2 * j + UK), g=fo[n],
                                      first=(j == 0), last=(j == nf - 1))))

    for j, us in fin:
        g = pl.group("ffn", (4, 5), us, j=j)
        mine = [("unit", u) for u in g["units"]]
        line.extend(mine[:2])
        if j >= 1:
            line.append(("turn_f", dict(j=j - 1, f=last_g)))
        line.extend(mine[2:])
        if j >= 1:
            add_out(j - 1)
        last_g = g
    line.append(("turn_f", dict(j=nf - 1, f=last_g)))
    add_out(nf - 1)
    line.append(("addnorm", dict(final=True)))
    pl.steps = lay_out(line)
    number(pl, pl.steps)
    return pl


def build(nc, A, out):
    W = dict(w_in=[A["w_in"][i] for i in range(DEPTH)], w_mem_kv=[A["w_mem_kv"][i] for i in range(DEPTH)],
             w_out=[A["w_out"][i] for i in range(DEPTH)])
    for name in ("w_in_2", "w_branch_swa_2", "w_branch_diff_2", "w_out_2", "w_ffn_in_2", "w_ffn_out_2"):
        W[name] = A[name][0]
    pl = make_plan(W)
    U, STEPS = pl.units, pl.steps
    cf_np, cb_np = constant_tables()
    cf_dram = nc.inline_tensor(cf_np, name="const_f32").ap()
    cb_dram = nc.inline_tensor(cb_np, name="const_masks").ap()

    ctx = ExitStack()
    with ctx:
        def sb(name, shape, dt=F32):
            return ctx.enter_context(nc.sbuf_tensor(name, shape, dt))

        def sem(name):
            return ctx.enter_context(nc.semaphore(name))

        psum = ctx.enter_context(nc.psum_tensor("psum", [P, 8, 512], F32))

        cf = sb("cf", [P, C_END])
        cb = sb("cb", [P, B_END], BF16)
        raw = sb("raw", [P, NSLOT, UK, 512])
        w_hi = sb("w_hi", [P, NSLOT, UK, 512], F32R)
        w_lo = sb("w_lo", [P, NSLOT, UK, 512], F32R)
        x = sb("x", [P, NT, D])
        xn = sb("xn", [P, NT, D])
        gates = sb("gates", [P, NT, 2 * D])
        S_hi = {"h": sb("h_hi", [P, KC, META + T], F32R), "m": sb("m_hi", [P, KC, T], F32R),
                "mix": sb("mix_hi", [P, KC, T], F32R)}
        S_lo = {"h": sb("h_lo", [P, KC, META + T], F32R), "m": sb("m_lo", [P, KC, T], F32R),
                "mix": sb("mix_lo", [P, KC, T], F32R)}
        S_hi["f"], S_lo["f"] = S_hi["m"], S_lo["m"]
        S_off = {"h": META, "m": 0, "mix": 0, "f": 0}
        gain = sb("gain", [P, NGAIN, D])
        stage = sb("stage", [P, NSTAGE, NT, 512])
        stage_m = sb("stage_m", [META, NSTAGE, 256])
        sgate = sb("sgate", [P, 2, NT, P])
        gtmp = sb("gtmp", [P, NT, P])
        qk = sb("qk", [P, 2, 784])
        probs = sb("probs", [P, 4, NT, 272])
        p_t = sb("p_t", [P, 2, 512])
        p_tm = sb("p_tm", [META, 2, NT * P])
        o_st = sb("o_st", [P, 2, NT, 256])
        sbt = sb("sbt", [P, 2, 384])
        rtmp = sb("rtmp", [P, 2, 5 * DH])
        stats = sb("stats", [P, 4, 8])
        rec = sb("rec", [P, 4, 4])
        nstat = sb("nstat", [P, 32])
        sinks = sb("sinks", [P, 32])
        lam_in = sb("lam_in", [P, 4, DH])
        lam = sb("lam", [P, 8])
        subln = sb("subln", [P, P])
        sil = sgate[:].rearrange("p i t n -> p (i t n)").rearrange("p (t n) -> p t n", t=NT)
        eps_col = sb("eps_col", [P, 1])
        hstat = sb("hstat", [P, 32])

        gflat = gates[:].rearrange("p t d -> p (t d)")
        mem_v = gflat[:, 0:NT * D].rearrange("p (t d) -> p t d", t=NT)
        mem_n = gflat[:, NT * D:2 * NT * D].rearrange("p (t d) -> p t d", t=NT)
        meta_v = gflat[0:META, 0:D]
        meta_n = gflat[0:META, D:2 * D]
        SRC = {"x": x, "xn": xn, "mem": mem_v, "mem_n": mem_n}

        mask_in = probs[:].rearrange("p j t k -> p (j t k)")[:, 0:B_END]
        TP, OB = 6, 7

        s_const = sem("s_const")
        s_x = sem("s_x")
        s_small = sem("s_small")
        s_meta = sem("s_meta")
        w_landed = [sem(f"w_landed{i}") for i in range(NSLOT)]
        s_gain = [sem(f"s_gain{i}") for i in range(NGAIN)]
        hi_ready = sem("hi_ready")
        lo_ready = sem("lo_ready")
        unit_used = sem("unit_used")
        group_done = sem("group_done")
        evac_act = sem("evac_act")
        evac_dve = sem("evac_dve")
        gate_e = sem("gate_e")
        gate_done = sem("gate_done")
        roped = sem("roped")
        turned = sem("turned")
        turned_hi = sem("turned_hi")
        tp_done = sem("tp_done")
        scores_done = sem("scores_done")
        negmax = sem("negmax")
        probs_ready = sem("probs_ready")
        sb_log = sem("sb_log")
        sb_soft = sem("sb_soft")
        sb_sum = sem("sb_sum")
        blended = sem("blended")
        out_done = sem("out_done")
        out_used = sem("out_used")
        ssq_ready = sem("ssq_ready")
        head_rstd = sem("head_rstd")
        norm_done = sem("norm_done")
        rstd_ready = sem("rstd_ready")
        silu_ready = sem("silu_ready")
        gate_bias = sem("gate_bias")
        gates_ready = sem("gates_ready")
        lam_sums = sem("lam_sums")
        lam_exp = sem("lam_exp")
        const_done = sem("const_done")
        dve_order = sem("dve_order")
        act_order = sem("act_order")
        pool_order = sem("pool_order")
        s_out = sem("s_out")

        SEM = dict(s_x=s_x, s_small=s_small, s_meta=s_meta, group_done=group_done, unit_used=unit_used,
                   evac_act=evac_act, evac_dve=evac_dve, norm_done=norm_done, tp_done=tp_done,
                   out_done=out_done, blended=blended)

        def wait(eng, what):
            if what is not None:
                eng.wait_ge(SEM[what[0]], what[1])

        def rows(w, c):
            return w[c * P:(c + UK) * P, :].rearrange("(k p) n -> p k n", p=P)

        gain_src = []
        for layer in range(DEPTH):
            gain_src += [A["norm_g"][layer:layer + 1, :], A["mem_norm_g"][layer:layer + 1, :]]
        gain_src += [A["final_norm_g"].rearrange("(a n) -> a n", a=1), A["pre_mix_gain_2"],
                     "same", A["b_gate_2"][:, 0:D], A["b_gate_2"][:, D:2 * D], A["post_mix_gain_2"],
                     A["pre_ffn_gain_2"], A["post_ffn_gain_2"]]
        gain_use = {}
        gk = 0
        gain_loads = []
        users = []
        for i, (what, s) in enumerate(STEPS):
            if what in ("norm", "metanorm", "addnorm") or (what == "evac" and s["g"]["kind"] == "gates"
                                                          and s["g"]["n"] % 2 == 0):
                if what == "metanorm":
                    gain_use[i] = gain_use[users[-1]]
                    users[-1] = i
                    gk += 1
                    continue
                n = len(gain_loads)
                gain_loads.append((gain_src[gk], n % NGAIN, 16 * (n // NGAIN + 1)))
                gain_use[i] = (n % NGAIN, 16 * (n // NGAIN + 1))
                users.append(i)
                gk += 1
                if what == "evac":
                    gate_gain = gain_use[i]
            elif what == "evac" and s["g"]["kind"] == "gates":
                gain_use[i] = gate_gain
                users[-1] = i
        assert gk == len(gain_src)
        gain_freed = []
        for i in users:
            what, s = STEPS[i]
            if what == "evac":
                gain_freed.append((evac_dve, s["g"]["free"][-1]))
            else:
                gain_freed.append((norm_done, s["done"][-1]))
        load_at = {}
        for n in range(NGAIN, len(gain_loads)):
            load_at.setdefault(users[n - NGAIN], []).append(n)

        def load_gain(eng, n):
            src, slot, _ = gain_loads[n]
            if n >= NGAIN:
                eng.wait_ge(*gain_freed[n - NGAIN])
            eng.dma_start(gain[:, slot, :], src.partition_broadcast(P).rearrange("p a n -> p (a n)"))\
               .then_inc(s_gain[slot], 16)

        def banks_free(eng, g):
            for prev in g["prev"]:
                if prev is not None and prev[0]["by"]:
                    eng.wait_ge(SEM[prev[0]["by"]], prev[0]["free"][prev[1]])

        def turn_aps(what, s):
            bank = TP if what == "turn_mix" else TP + s["batch"] % 2
            if what == "turn_norm":
                at = S_off[s["dest"]] + s["t"] * P
                name, c, n, lo, hi, width = s["dest"], s["c"], 4, at, at + P, P
            elif what == "turn_meta":
                name, c, n, lo, hi, width = "h", s["c"], 4, 0, META, META
            elif what == "turn_f":
                name, c, n, lo, hi, width = "f", (2 * s["j"]) % KC, 2, 0, T, T
            else:
                name, c = s["g"]["mix"][0]
                n, lo, hi, width = len(s["g"]["mix"]), 0, T, T
            src = psum[:, bank, 0:n * width].rearrange("p (c w) -> p c w", c=n)
            return (S_hi[name][:, c:c + n, lo:hi], S_lo[name][:, c:c + n, lo:hi]), src

        by_ga = {g["ga"]: g for g in pl.groups if "ga" in g}
        ffn_turned = [s["batch"] + 1 for what, s in STEPS if what == "turn_f"]

        block = ctx.enter_context(nc.Block())

        @block.sync
        def _(sp):
            sp.dma_start(x[:], A["x"][0].rearrange("(t p) d -> p t d", p=P)).then_inc(s_x, 16)
            sp.dma_start(cf[:], cf_dram).then_inc(s_const, 16)
            sp.dma_start(mask_in, cb_dram).then_inc(s_const, 16)
            for u in U:
                if u["u"] >= NSLOT:
                    sp.wait_ge(lo_ready, u["u"] - NSLOT + 1)
                for off, reps, w, c, c0, step, width in u["loads"]:
                    dst = raw[:, u["slot"], :, off:off + reps * width]
                    if reps == 1:
                        sp.dma_start(dst, rows(w, c)[:, :, c0:c0 + width]).then_inc(w_landed[u["slot"]], 16)
                    else:
                        for k in range(UK):
                            span = w[(c + k) * P:(c + k + 1) * P, c0:c0 + width].unsqueeze(1)
                            src = bass.AP(tensor=span.tensor, offset=span.offset,
                                          ap=[list(span.ap[0]), [step, reps], [1, width]])
                            sp.dma_start(dst[:, k, :].rearrange("p (i n) -> p i n", i=reps), src)\
                              .then_inc(w_landed[u["slot"]], 16)
            for t in range(NT):
                sp.wait_ge(norm_done, STEPS[-1][1]["done"][t])
                sp.dma_start(out[0, t * P:(t + 1) * P, :], x[:, t, :]).then_inc(s_out, 16)
            sp.wait_ge(s_out, 16 * NT)

        @block.gpsimd
        def _(pool):
            load_gain(pool, 0)
            pool.dma_start(mem_v, A["mem"][0].rearrange("(t p) d -> p t d", p=P)).then_inc(s_small, 16)
            load_gain(pool, 1)
            pool.dma_start(sinks[:, 0:16], A["attn_sink_2"].partition_broadcast(P)
                           .rearrange("p a n -> p (a n)")).then_inc(s_small, 16)
            for i, name in enumerate(("lambda_q1_2", "lambda_k1_2", "lambda_q2_2", "lambda_k2_2")):
                pool.dma_start(lam_in[:, i, :], A[name].partition_broadcast(P)
                               .rearrange("p a n -> p (a n)")).then_inc(s_small, 16)
            pool.dma_start(subln[:], A["diff_subln_gain_2"].partition_broadcast(P)
                           .rearrange("p a n -> p (a n)")).then_inc(s_small, 16)
            order = [0]

            def link(ins):
                order[0] += 1
                ins.then_inc(pool_order, 1)
                pool.wait_ge(pool_order, order[0])

            pool.wait_ge(s_const, 32)
            norms_seen = 0
            for i, (what, s) in enumerate(STEPS):
                if what in ("norm", "metanorm", "addnorm"):
                    norms_seen += 1
                    if norms_seen == 2 * DEPTH:
                        pool.wait_ge(norm_done, s["done"][-1])
                        pool.dma_start(meta_v, A["meta_tokens_2"]).then_inc(s_meta, 16)
                for n in load_at.get(i, []):
                    load_gain(pool, n)
                if what != "rope":
                    continue
                g = s["g"]
                st = stage[:, g["ga"] % NSTAGE]
                pool.wait_ge(evac_act, g["free"][-1])
                if g["kind"] == "mb":
                    v = st[:, :, 0:256].rearrange("p t (h d) -> p t h d", d=DH)
                    nh, w, half = 4, ROPE1, ROPE1 // 2
                    cos, sin = C_COS1, C_SIN1
                else:
                    nh = 5 if g["kind"] == "swa" else 4
                    v = st[:, :, 0:nh * DH].rearrange("p t (h d) -> p t h d", d=DH)
                    w, half = DH, DH // 2
                    cos, sin = C_COS2, C_SIN2
                a = rtmp[:, 0, 0:nh * w].rearrange("p (h d) -> p h d", h=nh)
                b = rtmp[:, 1, 0:nh * w].rearrange("p (h d) -> p h d", h=nh)
                ct = cf[:, cos:cos + NT * w].rearrange("p (t d) -> p t d", t=NT)
                sn = cf[:, sin:sin + NT * w].rearrange("p (t d) -> p t d", t=NT)
                for t in range(NT):
                    shape = [P, nh, w]
                    hs = [P, nh, half]
                    nc.gpsimd.tensor_tensor(a, v[:, t, :, 0:w], ct[:, t].unsqueeze(1).to_broadcast(shape),
                                            ALU.mult)
                    nc.gpsimd.tensor_tensor(b[:, :, 0:half], v[:, t, :, half:w],
                                            sn[:, t, 0:half].unsqueeze(1).to_broadcast(hs), ALU.mult)
                    link(nc.gpsimd.tensor_tensor(b[:, :, half:w], v[:, t, :, 0:half],
                                                 sn[:, t, half:w].unsqueeze(1).to_broadcast(hs), ALU.mult))
                    last = nc.gpsimd.tensor_tensor(v[:, t, :, 0:w], a, b, ALU.add)
                    if t < NT - 1:
                        link(last)
                if g["kind"] != "mb":
                    link(last)
                    nk = 1 if g["kind"] == "swa" else 2
                    sm = stage_m[:, g["ga"] % NSTAGE]
                    vm = sm[:, 0:nk * DH].rearrange("p (h d) -> p h d", d=DH)
                    am = rtmp[0:META, 0, 0:nk * DH].rearrange("p (h d) -> p h d", d=DH)
                    bm = rtmp[0:META, 1, 0:nk * DH].rearrange("p (h d) -> p h d", d=DH)
                    cm, smn = cf[0:META, C_COSM:C_COSM + DH], cf[0:META, C_SINM:C_SINM + DH]
                    nc.gpsimd.tensor_tensor(am, vm, cm.unsqueeze(1).to_broadcast([META, nk, DH]), ALU.mult)
                    nc.gpsimd.tensor_tensor(bm[:, :, 0:half], vm[:, :, half:DH],
                                            smn[:, 0:half].unsqueeze(1).to_broadcast([META, nk, half]), ALU.mult)
                    link(nc.gpsimd.tensor_tensor(bm[:, :, half:DH], vm[:, :, 0:half],
                                                 smn[:, half:DH].unsqueeze(1).to_broadcast([META, nk, half]),
                                                 ALU.mult))
                    last = nc.gpsimd.tensor_tensor(vm, am, bm, ALU.add)
                    if g["kind"] == "swa":
                        link(last)
                        nc.gpsimd.tensor_copy(st[:, :, 320:384], st[:, :, 256:320])
                        last = nc.gpsimd.tensor_copy(sm[:, DH:2 * DH], sm[:, 0:DH])
                last.then_inc(roped, 1)
                pool.wait_ge(roped, g["roped"])

        @block.tensor
        def _(pe):
            pe.wait_ge(const_done, 1)

            def turn(pairs):
                for o, i, n in pairs:
                    last = nc.tensor.transpose(o, i, cf[0:n, C_ID:C_ID + n])
                last.then_inc(tp_done, 1)

            where = {}
            for i, (what, s) in enumerate(STEPS):
                if what == "unit":
                    u, g = s, s["g"]
                    pe.wait_ge(hi_ready, u["u"] + 1)
                    pe.wait_ge(lo_ready, u["u"] + 1)
                    need = 0
                    for name, *_ in u["parts"]:
                        for c in range(*u["chunks"]):
                            need = max(need, where.get((name, c % KC if name == "f" else c), 0))
                    pe.wait_ge(turned, max(need, where["meta"]) if g.get("meta") else need)
                    if u["first"]:
                        banks_free(pe, g)
                    for t in range(NT):
                        bank = g["banks"][t]
                        for kk in range(UK):
                            for pi, (name, r0, r1, po) in enumerate(u["parts"]):
                                c = u["chunks"][0] + kk
                                c = c % KC if name == "f" else c
                                at = S_off[name] + t * P
                                n = r1 - r0
                                triples = ((S_hi, w_hi), (S_lo, w_hi), (S_hi, w_lo))
                                for z, (sx, wx) in enumerate(triples):
                                    first = u["first"] and kk == 0 and pi == 0 and z == 0
                                    end = u["last"] and kk == UK - 1 and z == 2
                                    last = nc.tensor.matmul(
                                        psum[:, bank, po:po + n], sx[name][:, c, at:at + P],
                                        wx[:, u["slot"], kk, r0:r1], start=first, stop=end,
                                        skip_group_check=True)
                            for r0, r1, mt, po in g.get("meta", []):
                                if mt != t:
                                    continue
                                c = u["chunks"][0] + kk
                                for z, (sx, wx) in enumerate(((S_hi, w_hi), (S_lo, w_hi), (S_hi, w_lo))):
                                    last = nc.tensor.matmul(
                                        psum[:, bank, po:po + r1 - r0], sx["h"][:, c, 0:P],
                                        wx[:, u["slot"], kk, r0:r1], start=False,
                                        stop=u["last"] and kk == UK - 1 and z == 2, skip_group_check=True)
                        if u["last"] and t == 0:
                            last.then_inc(group_done, 1)
                    last.then_inc(unit_used, 1)
                elif what in ("turn_norm", "turn_meta"):
                    b = s["batch"]
                    if b >= 2:
                        pe.wait_ge(turned, b if s["alone"] else b - 1)
                    if s["outs_before"]:
                        pe.wait_ge(out_used, s["outs_before"])
                    wait(pe, s["ready"])
                    bank = TP + b % 2
                    if what == "turn_norm":
                        src = SRC[s["source"]]
                        turn([(psum[:, bank, k * P:(k + 1) * P],
                                  src[:, s["t"], (s["c"] + k) * P:(s["c"] + k + 1) * P], P) for k in range(4)])
                        for k in range(4):
                            where[(s["dest"], s["c"] + k)] = b + 1
                    else:
                        turn([(psum[:, bank, k * META:(k + 1) * META],
                                  meta_n[:, (s["c"] + k) * P:(s["c"] + k + 1) * P], META) for k in range(4)])
                        where["meta"] = b + 1
                elif what == "turn_f":
                    b = s["batch"]
                    pe.wait_ge(turned, b - 1)
                    pe.wait_ge(evac_dve, s["f"]["free"][-1])
                    bank = TP + b % 2
                    turn([(psum[:, bank, (c * NT + t) * P:(c * NT + t + 1) * P],
                              o_st[:, s["j"] % 2, t, c * P:(c + 1) * P], P)
                             for c in range(2) for t in range(NT)])
                    for c in range(2):
                        where[("f", (2 * s["j"] + c) % KC)] = b + 1
                elif what == "turn_qk":
                    g = s["g"]
                    K = KINDS[g["kind"]]
                    st = stage[:, g["ga"] % NSTAGE]
                    if "roped" in g:
                        pe.wait_ge(roped, g["roped"])
                    pe.wait_ge(evac_act, g["free"][-1])
                    pe.wait_ge(turned, s["batch"])
                    if s["part"] == 0:
                        tiles = [(t, K["q"] + c * P) for c in range(K["qw"] // P) for t in range(NT)]
                        if g["kind"] in ("sb", "mb", "mem"):
                            tiles += [(t, K["k"]) for t in range(NT)]
                        turn([(psum[:, TP, n * P:(n + 1) * P], st[:, t, c0:c0 + P], P)
                              for n, (t, c0) in enumerate(tiles)])
                    else:
                        turn([(psum[:, TP, t * P:(t + 1) * P], st[:, t, K["k"]:K["k"] + P], P)
                              for t in range(NT)]
                             + [(psum[:, TP, T:T + META], stage_m[:, g["ga"] % NSTAGE, 0:P], META)])
                elif what == "scores":
                    g = s["g"]
                    kind, j, a = g["kind"], s["j"], s["a"]
                    pe.wait_ge(turned, g["qk_ready"])
                    if j >= 2:
                        pe.wait_ge(probs_ready, j - 1)
                    if s["meta_out"]:
                        pe.wait_ge(turned, s["meta_out"])
                    lo = 64 * (a % 2)
                    buf = qk[lo:lo + 64, g["ga"] % 2]
                    qoff = (a // 2) * T if kind == "swa" else 0
                    koff = 2 * P * (KINDS[kind]["qw"] // P)

                    def mm(o, l, r, start, stop=True):
                        return nc.tensor.matmul(o, l, r, start=start, stop=stop, skip_group_check=True)

                    idb = cb[:, B_ID:B_ID + P]
                    if kind == "sb":
                        S = psum[:, 4 + j % 2]
                        mm(S[:, 0:T], buf[:, koff:koff + P], buf[:, 0:T], True, False)
                        mm(S[:, T:T + P], buf[:, koff + P:koff + T], buf[:, P:T], False, False)
                        mm(S[:, 0:P], idb, cb[:, B_SB:B_SB + P], False, False)
                        last = mm(S[:, T:T + P], idb, cb[:, B_SB:B_SB + P], False, True)
                    elif kind == "mb":
                        S = psum[:, 4 + j % 2]
                        mm(S[:, 0:P], buf[:, 0:P], buf[:, koff:koff + P], True, False)
                        mm(S[:, T:2 * T], buf[:, P:T], buf[:, koff:koff + T], False, False)
                        mm(S[:, 0:P], idb, cb[:, B_LOW:B_LOW + P], False, False)
                        last = mm(S[:, T + P:2 * T], idb, cb[:, B_LOW:B_LOW + P], False, True)
                    elif kind == "mem":
                        S = psum[:, 4 + j % 2]
                        mm(S[:, 0:T], buf[:, 0:P], buf[:, koff:koff + T], True, False)
                        last = mm(S[:, T:2 * T], buf[:, P:T], buf[:, koff:koff + T], False, True)
                    else:
                        for t in range(NT):
                            S = psum[:, 2 + 2 * (j % 2) + t]
                            q = buf[:, qoff + t * P:qoff + (t + 1) * P]
                            last = mm(S[:, 0:T + META], q, buf[:, koff:koff + T + META], True, kind == "diff")
                            if kind == "swa":
                                m = B_LOW if t == 0 else B_UP
                                at = P if t == 0 else 0
                                last = mm(S[:, at:at + P], idb, cb[:, m:m + P], False, True)
                    last.then_inc(scores_done, 1)
                elif what == "later":
                    j = s["j"]
                    pe.wait_ge(sb_soft, s["sb"] + 1)
                    S = psum[:, 4 + j % 2]
                    r = sbt[:, j % 2]
                    nc.tensor.matmul(S[:, 0:384], cf[:, C_TRI:C_TRI + P], r[:, 0:384], start=False, stop=False,
                                     skip_group_check=True)
                    nc.tensor.matmul(S[:, P:T], cf[:, C_ONE:C_ONE + P], r[:, T:384], start=False, stop=True,
                                     skip_group_check=True).then_inc(sb_sum, 1)
                elif what == "turn_p":
                    g = s["g"]
                    kind, j, b = g["kind"], s["j"], s["batch"]
                    pe.wait_ge(turned, b)
                    if kind == "diff":
                        pe.wait_ge(blended, s["blended"])
                    else:
                        pe.wait_ge(probs_ready, j + 1)
                    pr = probs[:, j % 4]
                    blocks = [(0, 0), (1, 0), (1, 1)] if kind == "mb" else [(0, 0), (0, 1), (1, 0), (1, 1)]
                    todo = [(psum[:, TP, n * P:(n + 1) * P], pr[:, t, k * P:(k + 1) * P], P)
                            for n, (t, k) in enumerate(blocks)]
                    if kind in ("swa", "diff"):
                        todo += [(psum[0:META, 2 + 2 * (j % 2) + t, 384:512], pr[:, t, T:T + META], P)
                                 for t in range(NT)]
                    turn(todo)
                elif what == "out":
                    g = s["g"]
                    kind, j, o = g["kind"], s["j"], s["o"]
                    vs = stage[:, g["ga"] % NSTAGE]
                    vo = KINDS[kind]["v"]
                    if kind in ("swa", "diff"):
                        vm = stage_m[:, g["ga"] % NSTAGE, P:P + (DH if kind == "swa" else P)]
                    wide = P if kind == "diff" else DH
                    v0 = vo + (s["a"] * DH if kind in ("sb", "mb", "mem") else 0)
                    if kind == "sb":
                        pe.wait_ge(probs_ready, j + 1)
                        src = probs[:, j % 4].rearrange("p t k -> p (t k)")
                        blocks = [[(0, 0)], [(1, 0), (2, 1)]]
                    else:
                        pe.wait_ge(turned, s["batch"] + 1)
                        src = p_t[:, s["pt"] % 2]
                        blocks = {"mb": [[(0, 0)], [(1, 0), (2, 1)]]}.get(kind, [[(0, 0), (1, 1)], [(2, 0), (3, 1)]])
                    if o >= 1:
                        pe.wait_ge(out_used, o)
                    for t in range(NT):
                        dst = psum[:, OB, t * wide:(t + 1) * wide]
                        for n, (blk, kt) in enumerate(blocks[t]):
                            end = n == len(blocks[t]) - 1 and kind not in ("swa", "diff")
                            last = nc.tensor.matmul(dst, src[:, blk * P:(blk + 1) * P], vs[:, kt, v0:v0 + wide],
                                                    start=(n == 0), stop=end)
                        if kind in ("swa", "diff"):
                            last = nc.tensor.matmul(dst, p_tm[:, s["pt"] % 2, t * P:(t + 1) * P], vm,
                                                    start=False, stop=True)
                    last.then_inc(out_done, 1)
                elif what == "turn_mix":
                    g = s["g"]
                    b = s["batch"]
                    pe.wait_ge(turned, b)
                    pe.wait_ge(out_used, g["last_out"])
                    turn([(psum[:, TP, (c * NT + t) * P:(c * NT + t + 1) * P],
                              o_st[:, g["ga"] % 2, t, c * P:(c + 1) * P], P)
                             for c in range(len(g["mix"])) for t in range(NT)])
                    for name, c in g["mix"]:
                        where[(name, c)] = b + 1
                elif what == "settle":
                    pe.wait_ge(probs_ready, pl.count["jobs"])

        @block.scalar
        def _(act):
            order = [0]

            def link(ins):
                order[0] += 1
                ins.then_inc(act_order, 1)
                act.wait_ge(act_order, order[0])

            def split(u):
                act.wait_ge(w_landed[u["slot"]], u["landed"])
                if u["u"] >= NSLOT:
                    act.wait_ge(unit_used, u["u"] - NSLOT + 1)
                n = u["width"]
                nc.scalar.activation(w_hi[:, u["slot"], :, 0:n], raw[:, u["slot"], :, 0:n], ACT.Copy)\
                    .then_inc(hi_ready, 1)

            nc.scalar.preload_act_table_set("natural_log_exp_and_others")
            act.wait_ge(lam_sums, 1)
            nc.scalar.activation(lam[:, 2:4], lam[:, 0:2], ACT.Exp).then_inc(lam_exp, 1)
            for u in U[:SPLIT_AHEAD]:
                split(u)
            for i, (what, s) in enumerate(STEPS):
                if what == "unit":
                    for u in U[s["u"] + SPLIT_AHEAD:s["u"] + SPLIT_AHEAD + 1]:
                        split(u)
                elif what in ("norm", "addnorm", "metanorm"):
                    n = s["n"]
                    meta = what == "metanorm"
                    rowsn = META if meta else P
                    for t in range(1 if meta else NT):
                        wait(act, s["ready"][t])
                        if what == "norm":
                            srct, junk = SRC[s["source"]][:, t, :], (xn if s["source"] != "mem" else mem_n)[:, t, :]
                        elif meta:
                            srct, junk = meta_v, meta_n
                        else:
                            srct, junk = psum[:, 2 * t:2 * t + 2, :].rearrange("p b n -> p (b n)"), xn[:, t, :]
                        c = 4 * (n % 4) + 2 * t
                        ss = nstat[0:rowsn, c:c + 1]
                        rs = nstat[0:rowsn, 16 + c:17 + c]
                        link(nc.scalar.activation(junk, srct, ACT.Square, accum_out=ss))
                        link(nc.scalar.activation(ss, ss, ACT.Ln, scale=1.0 / D, bias=eps_col[0:rowsn, :]))
                        ins = nc.scalar.activation(rs, ss, ACT.Exp, scale=-0.5)
                        ins.then_inc(rstd_ready, 1)
                elif what in ("turn_norm", "turn_meta", "turn_f", "turn_mix"):
                    b = s["batch"]
                    act.wait_ge(tp_done, b + 1)
                    wait(act, s["dest_free"])
                    dst, src = turn_aps(what, s)
                    nc.scalar.activation(dst[0], src, ACT.Copy).then_inc(turned_hi, 1)
                elif what == "evac":
                    g = s["g"]
                    kind = g["kind"]
                    if kind in KINDS:
                        K = KINDS[kind]
                        st = stage[:, g["ga"] % NSTAGE]
                        if g["ga"] >= NSTAGE:
                            act.wait_ge(out_done, by_ga[g["ga"] - NSTAGE]["last_out"])
                        for t in range(NT):
                            wait(act, g["t_done"][t])
                            ps = psum[:, g["banks"][t]]
                            nc.scalar.activation(st[:, t, 0:K["qw"]], ps[:, 0:K["qw"]], ACT.Copy, scale=SCALE)
                            if kind == "swa":
                                last = nc.scalar.activation(
                                    st[:, t, 256:512].rearrange("p (i n) -> p i n", i=2)[:, :, 0:DH],
                                    ps[:, 256:384].rearrange("p (i n) -> p i n", i=2), ACT.Copy)
                                if t == 0:
                                    last = nc.scalar.activation(
                                        stage_m[:, g["ga"] % NSTAGE, 0:256].rearrange("p (i n) -> p i n", i=2)[:, :, 0:DH],
                                        ps[0:META, 384:512].rearrange("p (i n) -> p i n", i=2), ACT.Copy)
                            else:
                                last = nc.scalar.activation(st[:, t, K["qw"]:K["n"]], ps[:, K["qw"]:K["n"]], ACT.Copy)
                                if kind == "diff":
                                    last = nc.scalar.activation(
                                        stage_m[:, g["ga"] % NSTAGE, t * P:(t + 1) * P],
                                        ps[0:META, 384:512], ACT.Copy)
                            last.then_inc(evac_act, 1)
                    elif kind == "ffn":
                        for t in range(NT):
                            wait(act, g["t_done"][t])
                            if g["j"] >= 1:
                                act.wait_ge(evac_dve, g["free"][t] - NT)
                            nc.scalar.activation(sil[:, t, :], psum[:, g["banks"][t], 0:256], ACT.Silu)\
                                .then_inc(silu_ready, 1)
                    elif kind == "gates":
                        for t in range(NT):
                            act.wait_ge(evac_dve, g["free"][t])
                            gt = gates[:, t, g["n"] * 512:(g["n"] + 1) * 512]
                            nc.scalar.activation(gt, gt, ACT.Sigmoid).then_inc(gates_ready, 1)
                elif what == "gates_out":
                    nc.scalar.preload_act_table_set("natural_log_exp_and_others")
                elif what == "gate":
                    g = s["g"]
                    c0 = KINDS[g["kind"]]["g"]
                    act.wait_ge(evac_act, g["free"][-1])
                    if s["n"] >= 1:
                        act.wait_ge(gate_done, s["n"])
                    nc.scalar.activation(gtmp[:], stage[:, g["ga"] % NSTAGE, :, c0:c0 + P], ACT.Exp, scale=-1.0)\
                        .then_inc(gate_e, 1)
                elif what == "scores":
                    g = s["g"]
                    kind, j = g["kind"], s["j"]
                    wait(act, s["p_free"])
                    if kind == "sb":
                        S = psum[:, 4 + j % 2, 0:384]
                        pr = probs[:, j % 4].rearrange("p t k -> p (t k)")[:, 0:384]
                        act.wait_ge(scores_done, j + 1)
                        link(nc.scalar.activation(pr, S, ACT.Abs))
                        link(nc.scalar.activation(pr, pr, ACT.Exp, scale=-1.0))
                        nc.scalar.activation(pr, pr, ACT.Ln, bias=1.0).then_inc(sb_log, 1)
                    else:
                        act.wait_ge(negmax, s["soft"] + 1)
                        stt = stats[:, j % 4]
                        for t in range(NT):
                            if kind in ("mb", "mem"):
                                n = P if (kind == "mb" and t == 0) else T
                                src = psum[:, 4 + j % 2, t * T:t * T + n]
                            else:
                                n = T + META
                                src = psum[:, 2 + 2 * (j % 2) + t, 0:n]
                            last = nc.scalar.activation(probs[:, j % 4, t, 0:n], src, ACT.Exp,
                                                        bias=stt[:, t:t + 1], accum_out=stt[:, 2 + t:3 + t])
                        if kind == "swa":
                            last = nc.scalar.activation(stt[:, 6:8], stt[:, 4:6], ACT.Exp)
                        last.then_inc(probs_ready, 1)
                elif what == "later":
                    j = s["j"]
                    act.wait_ge(sb_sum, s["sb"] + 1)
                    pr = probs[:, j % 4].rearrange("p t k -> p (t k)")[:, 0:384]
                    nc.scalar.activation(pr, psum[:, 4 + j % 2, 0:384], ACT.Exp).then_inc(probs_ready, 1)
                elif what == "out" and s["g"]["kind"] == "diff":
                    act.wait_ge(out_done, s["o"] + 1)
                    d = s["g"]["d"]
                    c = 4 * (d % 4)
                    for t in range(NT):
                        last = nc.scalar.activation(sil[:, t, 0:P], psum[:, OB, t * P:(t + 1) * P], ACT.Square,
                                                    accum_out=hstat[:, c + t:c + t + 1])
                    link(last)
                    link(nc.scalar.activation(hstat[:, c + 2:c + 4], hstat[:, c:c + 2], ACT.Ln, scale=1.0 / P,
                                              bias=eps_col[:, :]))
                    nc.scalar.activation(hstat[:, 16 + c:18 + c], hstat[:, c + 2:c + 4], ACT.Exp, scale=-0.5)\
                        .then_inc(head_rstd, 1)

        @block.vector
        def _(dve):
            order = [0]

            def link(ins):
                order[0] += 1
                ins.then_inc(dve_order, 1)
                dve.wait_ge(dve_order, order[0])

            def split(u):
                dve.wait_ge(w_landed[u["slot"]], u["landed"])
                dve.wait_ge(hi_ready, u["u"] + 1)
                if u["u"] >= NSLOT:
                    dve.wait_ge(unit_used, u["u"] - NSLOT + 1)
                n = u["width"]
                nc.vector.tensor_tensor(w_lo[:, u["slot"], :, 0:n], raw[:, u["slot"], :, 0:n],
                                        w_hi[:, u["slot"], :, 0:n].bitcast(F32), ALU.subtract)\
                    .then_inc(lo_ready, 1)

            link(nc.vector.memset(eps_col[:], EPS))
            dve.wait_ge(s_const, 32)
            nc.vector.tensor_copy(cb[:], mask_in).then_inc(const_done, 1)
            dve.wait_ge(s_small, 16 * SMALL)
            for i in range(2):
                link(nc.vector.tensor_tensor(lam_in[:, 2 * i, :], lam_in[:, 2 * i, :], lam_in[:, 2 * i + 1, :],
                                             ALU.mult))
            nc.vector.tensor_reduce(lam[:, 0:1], lam_in[:, 0, :], AX.X, ALU.add)
            nc.vector.tensor_reduce(lam[:, 1:2], lam_in[:, 2, :], AX.X, ALU.add).then_inc(lam_sums, 1)
            nc.vector.tensor_scalar(sinks[:, 16:32], sinks[:, 0:16], -1.0, None, ALU.mult)
            link(nc.vector.tensor_scalar(subln[:], subln[:], 1.0 - LAMBDA_INIT, None, ALU.mult))
            dve.wait_ge(lam_exp, 1)
            link(nc.vector.tensor_tensor(lam[:, 4:5], lam[:, 2:3], lam[:, 3:4], ALU.subtract))
            link(nc.vector.tensor_scalar(lam[:, 5:6], lam[:, 4:5], LAMBDA_INIT, None, ALU.add))
            for u in U[:SPLIT_AHEAD]:
                split(u)
            for i, (what, s) in enumerate(STEPS):
                if what == "unit":
                    for u in U[s["u"] + SPLIT_AHEAD:s["u"] + SPLIT_AHEAD + 1]:
                        split(u)
                elif what in ("norm", "addnorm", "metanorm"):
                    n = s["n"]
                    meta = what == "metanorm"
                    rowsn = META if meta else P
                    dve.wait_ge(s_gain[gain_use[i][0]], gain_use[i][1])
                    gn = gain[0:rowsn, gain_use[i][0], :]
                    for t in range(1 if meta else NT):
                        dve.wait_ge(rstd_ready, s["rstd"][t])
                        c = 4 * (n % 4) + 2 * t
                        rs = nstat[0:rowsn, 16 + c:17 + c]
                        if what == "norm":
                            srct, dst = SRC[s["source"]][:, t, :], SRC[s["dest"]][:, t, :]
                        elif meta:
                            srct, dst = meta_v, meta_n
                        else:
                            srct, dst = psum[:, 2 * t:2 * t + 2, :].rearrange("p b n -> p (b n)"), xn[:, t, :]
                        ins = nc.vector.scalar_tensor_tensor(out=dst, in0=srct, scalar=rs, in1=gn,
                                                             op0=ALU.mult, op1=ALU.mult)
                        if what == "addnorm":
                            link(ins)
                            ins = nc.vector.tensor_tensor(x[:, t, :], x[:, t, :], xn[:, t, :], ALU.add)
                        ins.then_inc(norm_done, 1)
                elif what in ("turn_norm", "turn_meta", "turn_f", "turn_mix"):
                    b = s["batch"]
                    dve.wait_ge(turned_hi, s["half"])
                    dst, src = turn_aps(what, s)
                    nc.vector.tensor_tensor(dst[1], src, dst[0].bitcast(F32), ALU.subtract).then_inc(turned, 1)
                elif what == "turn_qk":
                    g = s["g"]
                    if g["ga"] >= 2:
                        dve.wait_ge(scores_done, by_ga[g["ga"] - 2]["last_scores"])
                    q_n = NT * P * (KINDS[g["kind"]]["qw"] // P)
                    two = g["kind"] in ("swa", "diff")
                    dve.wait_ge(tp_done, s["batch"] + 1)
                    n0 = q_n if two else q_n + T
                    if s["part"] == 0:
                        nc.vector.tensor_copy(qk[:, g["ga"] % 2, 0:n0], psum[:, TP, 0:n0]).then_inc(turned, 1)
                    else:
                        nc.vector.tensor_copy(qk[:, g["ga"] % 2, q_n:q_n + T + META], psum[:, TP, 0:T + META])\
                            .then_inc(turned, 1)
                elif what == "gate":
                    g = s["g"]
                    c0 = KINDS[g["kind"]]["g"]
                    dve.wait_ge(gate_e, s["n"] + 1)
                    link(nc.vector.tensor_scalar(gtmp[:], gtmp[:], 1.0, None, ALU.add))
                    link(nc.vector.reciprocal(gtmp[:], gtmp[:]))
                    nc.vector.tensor_tensor(sgate[:, g["ga"] % 2], gtmp[:], stage[:, g["ga"] % NSTAGE, :, c0:c0 + P],
                                            ALU.mult).then_inc(gate_done, 1)
                    dve.wait_ge(gate_done, s["n"] + 1)
                elif what == "scores":
                    g = s["g"]
                    kind, j = g["kind"], s["j"]
                    stt = stats[:, j % 4]
                    if kind == "sb":
                        dve.wait_ge(sb_log, s["sb"] + 1)
                        if s["sb"] >= 2:
                            dve.wait_ge(sb_sum, s["sb"] - 1)
                        nc.vector.scalar_tensor_tensor(
                            out=sbt[:, j % 2], in0=psum[:, 4 + j % 2, 0:384], scalar=0.0,
                            in1=probs[:, j % 4].rearrange("p t k -> p (t k)")[:, 0:384],
                            op0=ALU.max, op1=ALU.add).then_inc(sb_soft, 1)
                        continue
                    dve.wait_ge(scores_done, j + 1)
                    if j >= 4:
                        dve.wait_ge(probs_ready, j - 3)
                    if kind == "mb":
                        nc.vector.tensor_reduce(stt[:, 0:1], psum[:, 4 + j % 2, 0:P], AX.X, ALU.max, negate=True)
                        last = nc.vector.tensor_reduce(stt[:, 1:2], psum[:, 4 + j % 2, T:2 * T], AX.X, ALU.max,
                                                       negate=True)
                    elif kind == "mem":
                        last = nc.vector.tensor_reduce(
                            stt[:, 0:2], psum[:, 4 + j % 2].rearrange("p (t k) -> p t k", t=NT), AX.X, ALU.max,
                            negate=True)
                    else:
                        b0 = 2 + 2 * (j % 2)
                        last = nc.vector.tensor_reduce(stt[:, 0:2], psum[:, b0:b0 + 2, 0:T + META], AX.X, ALU.max,
                                                       negate=True)
                        if kind == "swa":
                            hd = g["kv"] * 4 + s["a"]
                            link(last)
                            link(nc.vector.tensor_scalar(stt[:, 0:2], stt[:, 0:2], sinks[:, 16 + hd:17 + hd], None,
                                                         ALU.min))
                            last = nc.vector.tensor_scalar(stt[:, 4:6], stt[:, 0:2], sinks[:, hd:hd + 1], None,
                                                           ALU.add)
                    last.then_inc(negmax, 1)
                elif what == "blend":
                    j0 = s["j"]
                    j1 = j0 + 1
                    dve.wait_ge(probs_ready, j1 + 1)
                    nc.vector.reciprocal(rec[:, j0 % 4, 0:2], stats[:, j0 % 4, 2:4])
                    link(nc.vector.reciprocal(rec[:, j1 % 4, 0:2], stats[:, j1 % 4, 2:4]))
                    link(nc.vector.tensor_scalar(rec[:, j1 % 4, 0:2], rec[:, j1 % 4, 0:2], lam[:, 5:6], None, ALU.mult))
                    nc.vector.tensor_scalar(probs[:, j1 % 4, 0, :], probs[:, j1 % 4, 0, :], rec[:, j1 % 4, 0:1],
                                            None, ALU.mult)
                    link(nc.vector.tensor_scalar(probs[:, j1 % 4, 1, :], probs[:, j1 % 4, 1, :], rec[:, j1 % 4, 1:2],
                                                 None, ALU.mult))
                    for t in range(NT):
                        last = nc.vector.scalar_tensor_tensor(
                            out=probs[:, j0 % 4, t, :], in0=probs[:, j0 % 4, t, :], scalar=rec[:, j0 % 4, t:t + 1],
                            in1=probs[:, j1 % 4, t, :], op0=ALU.mult, op1=ALU.subtract)
                    last.then_inc(blended, 1)
                elif what == "turn_p":
                    g = s["g"]
                    kind = g["kind"]
                    dve.wait_ge(tp_done, s["batch"] + 1)
                    if s["pt"] >= 2:
                        dve.wait_ge(out_done, s["pt_free"])
                    n = 384 if kind == "mb" else 512
                    last = nc.vector.tensor_copy(p_t[:, s["pt"] % 2, 0:n], psum[:, TP, 0:n])
                    if kind in ("swa", "diff"):
                        b0 = 2 + 2 * (s["j"] % 2)
                        last = nc.vector.tensor_copy(p_tm[:, s["pt"] % 2, :].rearrange("p (t q) -> p t q", t=NT), psum[0:META, b0:b0 + 2, 384:512])
                    last.then_inc(turned, 1)
                elif what == "out":
                    g = s["g"]
                    kind, j, o, a = g["kind"], s["j"], s["o"], s["a"]
                    st = o_st[:, g["ga"] % 2]
                    if s["first_out"] and g["ga"] >= 2:
                        dve.wait_ge(tp_done, by_ga[g["ga"] - 2]["mixed"])
                    if kind in ("mb", "mem", "swa"):
                        dve.wait_ge(probs_ready, j + 1)
                        if kind == "swa":
                            link(nc.vector.tensor_tensor(stats[:, j % 4, 2:4], stats[:, j % 4, 2:4],
                                                         stats[:, j % 4, 6:8], ALU.add))
                        link(nc.vector.reciprocal(rec[:, j % 4, 0:2], stats[:, j % 4, 2:4]))
                    dve.wait_ge(out_done, o + 1)
                    if kind == "sb":
                        last = nc.vector.tensor_tensor(
                            st[:, :, a * DH:(a + 1) * DH],
                            psum[:, OB, 0:NT * DH].rearrange("p (t d) -> p t d", t=NT),
                            sgate[:, g["ga"] % 2, :, a * DH:(a + 1) * DH], ALU.mult)
                    elif kind in ("mb", "mem"):
                        for t in range(NT):
                            last = nc.vector.scalar_tensor_tensor(
                                out=st[:, t, a * DH:(a + 1) * DH], in0=psum[:, OB, t * DH:(t + 1) * DH],
                                scalar=rec[:, j % 4, t:t + 1], in1=sgate[:, g["ga"] % 2, t, a * DH:(a + 1) * DH],
                                op0=ALU.mult, op1=ALU.mult)
                    elif kind == "swa":
                        for t in range(NT):
                            last = nc.vector.tensor_scalar(st[:, t, a * DH:(a + 1) * DH],
                                                           psum[:, OB, t * DH:(t + 1) * DH],
                                                           rec[:, j % 4, t:t + 1], None, ALU.mult)
                    else:
                        d = g["d"]
                        c = 4 * (d % 4)
                        dve.wait_ge(head_rstd, d + 1)
                        for t in range(NT):
                            last = nc.vector.scalar_tensor_tensor(
                                out=st[:, t, 0:P], in0=psum[:, OB, t * P:(t + 1) * P],
                                scalar=hstat[:, 16 + c + t:17 + c + t], in1=subln[:], op0=ALU.mult, op1=ALU.mult)
                    last.then_inc(out_used, 1)
                elif what == "evac":
                    g = s["g"]
                    kind = g["kind"]
                    if kind in KINDS:
                        continue
                    if kind == "gates":
                        dve.wait_ge(s_gain[gain_use[i][0]], gain_use[i][1])
                    for t in range(NT):
                        ps = psum[:, g["banks"][t]]
                        wait(dve, g["t_done"][t])
                        if kind == "wo":
                            xs = x[:, t, g["n"] * 512:(g["n"] + 1) * 512]
                            last = nc.vector.tensor_tensor(xs, xs, ps, ALU.add)
                        elif kind == "gates":
                            n = g["n"]
                            last = nc.vector.tensor_tensor(gates[:, t, n * 512:(n + 1) * 512], ps,
                                                           gain[:, gain_use[i][0], (n % 2) * 512:(n % 2) * 512 + 512],
                                                           ALU.add)
                        elif kind in ("bswa", "bdiff"):
                            n = g["n"]
                            if kind == "bswa":
                                dve.wait_ge(gates_ready, NT * 4)
                                last = nc.vector.tensor_tensor(xn[:, t, n * 512:(n + 1) * 512], ps,
                                                               gates[:, t, n * 512:(n + 1) * 512], ALU.mult)
                            else:
                                gt = gates[:, t, D + n * 512:D + (n + 1) * 512]
                                link(nc.vector.tensor_tensor(gt, ps, gt, ALU.mult))
                                xs = xn[:, t, n * 512:(n + 1) * 512]
                                last = nc.vector.tensor_tensor(xs, xs, gt, ALU.add)
                        elif kind == "ffn":
                            dve.wait_ge(silu_ready, NT * g["j"] + t + 1)
                            if g["j"] >= 2 and t == 0:
                                dve.wait_ge(tp_done, ffn_turned[g["j"] - 2])
                            last = nc.vector.tensor_tensor(o_st[:, g["j"] % 2, t, :], ps[:, 256:512], sil[:, t, :],
                                                           ALU.mult)
                        last.then_inc(evac_dve, 1)


_INS = ["x", "mem", "norm_g", "w_in", "mem_norm_g", "w_mem_kv", "w_out", "final_norm_g", "meta_tokens_2",
        "pre_mix_gain_2", "w_in_2", "b_gate_2", "attn_sink_2", "lambda_q1_2", "lambda_k1_2", "lambda_q2_2",
        "lambda_k2_2", "diff_subln_gain_2", "w_branch_swa_2", "w_branch_diff_2", "w_out_2", "post_mix_gain_2",
        "pre_ffn_gain_2", "w_ffn_in_2", "w_ffn_out_2", "post_ffn_gain_2"]


def kernel(**inputs):
    import numpy as _np
    import concourse.bacc as _bacc
    from concourse import mybir as _mybir
    from concourse.bass_utils import run_bass_kernel_spmd as _run

    nc = _bacc.Bacc("TRN2", target_bir_lowering=False, num_devices=1)
    arrays, args = {}, {}
    for name in _INS:
        a = _np.ascontiguousarray(inputs[name])
        arrays[f"in_{name}"] = a
        args[name] = nc.dram_tensor(f"in_{name}", a.shape, _mybir.dt.from_np(a.dtype), kind="ExternalInput").ap()
    out = nc.dram_tensor("out", (1, T, D), F32, kind="ExternalOutput").ap()
    build(nc, args, out)
    r = _run(nc, [arrays], core_ids=[0])
    return r.results[0]["out"]
```

```python
import math
from contextlib import ExitStack

import numpy as np

import concourse.bass as bass
from concourse import mybir

F32 = mybir.dt.float32
F32R = mybir.dt.float32r
BF16 = mybir.dt.bfloat16
ACT = mybir.ActivationFunctionType
ALU = mybir.AluOpType
AX = mybir.AxisListType

P = 128
D = 1024
T = 256
NT = T // P
KC = D // P
DEPTH = 2
DH = 64
MEM_HEADS = 4
MEMW = MEM_HEADS * DH
SBW = (D - MEMW) // 2
ROPE1 = DH // 4
THETA1, THETA2 = 500000.0, 10000.0
EPS = 1e-6
NEG = -1e30
META = 16
KVH = 4
QA, KA, VA = 1024, 256, 256
QB = KB = VB = 1024
IN2 = QA + KA + VA + QB + KB + VB + 2 * D
DIFF_HEADS = 8
DFF = ((8 * D // 3 + 255) // 256) * 256
LAMBDA_INIT = 0.8 - 0.6 * math.exp(-0.3 * 0)
SCALE = DH ** -0.5

NSLOT = 5
NRAW = 4
UK = 2
NSTAGE = 3
NGAIN = 2
SMALL_BANK = 6
SMALL = 6
SPLIT_AHEAD = 3
SPLIT_LAST = ("diff", "mb", "wo", "bswa", "mkv")

C_ID, C_TRI, C_ONE = 0, 128, 256
C_COS1 = 384
C_SIN1 = C_COS1 + NT * ROPE1
C_COS2 = C_SIN1 + NT * ROPE1
C_SIN2 = C_COS2 + NT * DH
C_COSM = C_SIN2 + NT * DH
C_SINM = C_COSM + DH
C_END = C_SINM + DH
B_ID, B_SB, B_LOW, B_UP, B_END = 0, 128, 256, 384, 512


def constant_tables():
    f = np.zeros((P, C_END), np.float32)
    j = np.arange(P)
    f[:, C_ID:C_ID + P] = np.eye(P)
    f[:, C_TRI:C_TRI + P] = -(j[:, None] >= j[None, :]).astype(np.float32)
    f[:, C_ONE:C_ONE + P] = -1.0

    def angles(pos, theta, dims):
        inv = np.float32(theta) ** (-np.arange(dims // 2, dtype=np.float32) * np.float32(2.0)
                                    / np.float32(dims))
        a = pos.astype(np.float32)[:, None] * inv.astype(np.float32)[None, :]
        c, s = np.cos(a.astype(np.float64)), np.sin(a.astype(np.float64))
        return np.concatenate([c, c], 1), np.concatenate([-s, s], 1)

    for t in range(NT):
        c, s = angles(t * P + j, THETA1, ROPE1)
        f[:, C_COS1 + t * ROPE1:C_COS1 + (t + 1) * ROPE1] = c
        f[:, C_SIN1 + t * ROPE1:C_SIN1 + (t + 1) * ROPE1] = s
        c, s = angles(META + t * P + j, THETA2, DH)
        f[:, C_COS2 + t * DH:C_COS2 + (t + 1) * DH] = c
        f[:, C_SIN2 + t * DH:C_SIN2 + (t + 1) * DH] = s
    c, s = angles(np.arange(META), THETA2, DH)
    f[:META, C_COSM:C_COSM + DH] = c
    f[:META, C_SINM:C_SINM + DH] = s
    b = np.zeros((P, B_END), np.float32)
    b[:, B_ID:B_ID + P] = np.eye(P)
    r, c = j[:, None], j[None, :]
    b[:, B_SB:B_SB + P] = np.where(r < c, 0.0, NEG)
    b[:, B_LOW:B_LOW + P] = np.where(c <= r, 0.0, NEG)
    b[:, B_UP:B_UP + P] = np.where(r <= c, 0.0, NEG)
    return f, b


KINDS = {
    "sb": dict(n=512, q=0, k=128, v=256, g=384, heads=2, qw=128),
    "mb": dict(n=512, q=0, k=128, v=256, g=384, heads=2, qw=128),
    "mem": dict(n=512, q=0, g=256, heads=4, qw=256),
    "swa": dict(n=384, q=0, k=256, v=384, heads=4, qw=256),
    "diff": dict(n=384, q=0, k=128, v=256, heads=1, qw=128),
}


class Plan:

    def __init__(self):
        self.groups, self.steps, self.units = [], [], []
        self.bank_user = {}
        self.count = dict.fromkeys(("attn", "evac_act", "evac_dve", "jobs", "softs", "sbs", "outs", "batches",
                                    "his", "gated", "roped", "pts", "blends", "norms", "rstd", "norm_done",
                                    "groups", "silus", "turns"), 0)

    def next(self, name, n=1):
        self.count[name] += n
        return self.count[name]

    def group(self, kind, banks, units, **kw):
        g = dict(kind=kind, banks=banks, t_done=[], free=[], **kw)
        if kind in KINDS:
            g["ga"] = self.next("attn") - 1
            g["by"] = "evac_act"
        elif kind in ("mkv", "metakv"):
            g["by"] = "evac_act"
        else:
            g["by"] = None if kind in ("wo2", "fout") else "evac_dve"
        g["prev"] = [self.bank_user.get(b) for b in banks]
        for t, b in enumerate(banks):
            self.bank_user[b] = (g, t)
        g["units"] = [dict(loads=loads, operand=operand, chunks=chunks, g=g, first=(n == 0),
                           last=(n == len(units) - 1))
                      for n, (chunks, loads, operand) in enumerate(units)]
        self.groups.append(g)
        return g


SLOTS = {
    "sb": dict(turn_qk=(1,), gate=(1.25, 2.25), scores=(3, 3), later=(4, 4.5), out=(7.75, 7.5),
               turn_mix=(9,)),
    "mb": dict(turn_qk=(2.5,), gate=(2.25, 4.25), scores=(3, 4), turn_p=(4.5, 5), out=(5.5, 7),
               turn_mix=(7.5,)),
    "mem": dict(turn_qk=(1,), gate=(0.25, 2.25), scores=(1.75, 3.75, 3.75, 5.75), turn_p=(4, 6, 7, 7.75),
                out=(5.75, 6.75, 7.75, 8.75), turn_mix=(11.5,)),
    "swa": dict(turn_qk=(3.25, 2.75), scores=(4.75, 6.75, 6.75, 7.75), turn_p=(6.25, 7.25, 8.25, 9.25),
                out=(6.75, 8.25, 9.25, 10.5), turn_mix=(11.75,)),
    "diff": dict(turn_qk=(1.5, 2.5), scores=(4.25, 6), blend=(6.25,), turn_p=(7.75,), out=(8.75,),
                 turn_mix=(9.75,)),
}


def attention_slots(g):
    slots = {}
    jobs = [dict(g=g, a=a) for a in range(4)]
    for what, places in SLOTS[g["kind"]].items():
        for n, at in enumerate(places):
            if what == "turn_qk":
                s = dict(g=g, part=n)
            elif what == "gate":
                s = dict(g=g, t=n)
            elif what == "turn_mix":
                s = dict(g=g)
            else:
                s = jobs[n]
            slots.setdefault(at, []).append((what, s))
    return slots


def lay_out(timeline):
    due, steps = {}, []
    clock = 0.0
    order = []
    for what, arg in timeline:
        if what in ("unit", "unit_a") or (what == "unit_b" and arg["g"]["kind"] == "metakv"):
            order.append(arg)
    begun = ended = split = 0

    def splits(most=len(order)):
        nonlocal split
        while split < most and split < begun + SPLIT_AHEAD and split < ended + NSLOT:
            steps.append(("split", order[split]))
            split += 1

    def part(name, u):
        nonlocal clock, begun, ended
        g = u["g"]
        tile = 0 if name == "unit" or g["kind"] == "metakv" else 1
        if tile == 0:
            assert order[begun] is u
            begun += 1
        steps.append((name, u))
        if name == "unit_end":
            assert order[ended] is u
            ended += 1
        if g["kind"] not in SPLIT_LAST:
            splits()
        if u["last"] and (g["by"] or g["kind"] == "gates"):
            steps.append(("evac", dict(g=g, t=tile)))
            if g["kind"] in ("mb", "swa", "diff") and tile == 1:
                steps.append(("rope", dict(g=g)))
        if u["last"] and g["kind"] in KINDS and name == "unit_end":
            for at, some in attention_slots(g).items():
                due.setdefault(clock + 0.5 + at, []).extend(some)
        clock += 0.5
        for k in sorted(k for k in due if k <= clock):
            steps.extend(due.pop(k))
        if g["kind"] in SPLIT_LAST:
            splits()

    for what, arg in timeline:
        if what == "splits":
            splits(arg)
        elif what == "unit":
            if arg["g"]["kind"] != "metakv":
                part("unit", arg)
            part("unit_end", arg)
        elif what == "unit_a":
            part("unit", arg)
        elif what == "unit_b":
            part("unit_end", arg)
        elif what == "flush":
            for k in sorted(due):
                steps.extend(due[k])
            due = {}
        else:
            steps.append((what, arg))
    assert not due and begun == ended == split == len(order)
    return steps


def number(pl, steps):
    slot_dmas = [0] * NRAW
    reader = {}
    probs_reader = {}
    outs_of_pt = []
    meta_turned = {}
    x_ready = [(f"s_x{t}", 16) for t in range(NT)]
    xn_ready = {}
    mem_ready = [("s_mem", 16)] * NT
    ring_free = []
    last_mem = None
    km_ready = 0
    other_ready = {}
    gate_before = {}
    product_done = {}

    def ring(s, free, of=""):
        n = len(ring_free)
        s[of + "bank"] = SMALL_BANK + n % 2
        s[of + "bank_free"] = ring_free[n - 2] if n >= 2 else None
        ring_free.append(free)

    for what, s in steps:
        g = s.get("g") if isinstance(s, dict) else None
        if what in ("unit", "unit_end"):
            tile = 0 if what == "unit" or g["kind"] == "metakv" else 1
            for c in range(*s["chunks"]):
                reader[(s["operand"] if s["operand"] != "f" else "m", c % KC, tile)] = s
            if what == "unit_end":
                s["ended"] = True
            if s["last"]:
                if tile or g["kind"] == "metakv":
                    g["t_done"].append(("unit_used", s["u"] + 1))
                else:
                    g["t_done"].append(("group_done", pl.next("groups")))
                if g["kind"] in ("wo2", "fout"):
                    product_done[tile] = g["t_done"][tile]
        elif what == "split":
            u = len(pl.units)
            s["u"], s["slot"], s["raw"] = u, u % NSLOT, u % NRAW
            slot_dmas[s["raw"]] += 16 * sum(1 if load[1] == 1 else UK for load in s["loads"])
            s["landed"] = slot_dmas[s["raw"]]
            s["width"] = sum(reps * width for _, reps, _, _, _, _, width in s["loads"])
            pl.units.append(s)
        elif what == "evac":
            t = s["t"]
            g["free"].append(pl.next(g["by"]))
            if g["kind"] == "mkv":
                s["mem_before"] = last_mem
            if g["kind"] == "wo":
                x_ready[t] = ("evac_dve", g["free"][t])
            elif g["kind"] == "metakv":
                meta_kv_ready = g["free"][-1]
            elif g["kind"] == "bdiff":
                xn_ready[(g["n"], t)] = ("evac_dve", g["free"][t])
            elif g["kind"] == "ffn":
                g["silu"] = g.get("silu", []) + [pl.next("silus")]
        elif what == "rope":
            g["roped"] = pl.next("roped")
        elif what == "rope_meta":
            s["roped"] = pl.next("roped")
            s["ready"] = meta_kv_ready
        elif what == "gate":
            s["n"] = pl.next("gated") - 1
            s["before"] = gate_before.get(s["t"])
            gate_before[s["t"]] = s["n"] + 1
        elif what == "scores":
            s["j"] = j = pl.next("jobs") - 1
            s["p_free"] = probs_reader.get(j % 4)
            s["meta_out"] = meta_turned.get(j % 2)
            if g["kind"] == "sb":
                s["sb"] = pl.next("sbs") - 1
            else:
                s["soft"] = pl.next("softs") - 1
            if g["kind"] == "mem":
                g["km_ready"] = km_ready
            g["last_scores"] = j + 1
        elif what == "turn_qk":
            s["batch"] = pl.next("batches") - 1
            s["turned"] = pl.next("turns")
            ring(s, ("turned", s["turned"]))
            g["qk_ready"] = s["turned"]
        elif what == "turn_mk":
            s["batch"] = pl.next("batches") - 1
            s["turned"] = pl.next("turns")
            ring(s, ("turned", s["turned"]))
            km_ready = s["turned"]
            s["mem_before"] = last_mem
        elif what == "blend":
            s["blended"] = pl.next("blends")
            probs_reader[(s["j"] + 1) % 4] = ("blended", s["blended"])
        elif what == "turn_p":
            s["batch"] = pl.next("batches") - 1
            s["pt"] = pl.next("pts") - 1
            ring(s, ("pt_ready", s["pt"] + 1))
            s["pt_free"] = outs_of_pt[s["pt"] - 2] if s["pt"] >= 2 else None
            probs_reader[s["j"] % 4] = ("tp_done", s["batch"] + 1)
            if g["kind"] in ("swa", "diff"):
                meta_turned[s["j"] % 2] = s["pt"] + 1
        elif what == "out":
            s["o"] = pl.next("outs") - 1
            ring(s, ("out_used", s["o"] + 1), "out_")
            if g["kind"] == "mem":
                last_mem = g
            s["first_out"] = "last_out" not in g
            g["last_out"] = s["o"] + 1
            if g["kind"] == "sb":
                probs_reader[s["j"] % 4] = ("out_done", s["o"] + 1)
            else:
                outs_of_pt.append(s["o"] + 1)
        elif what in ("norm", "addnorm", "metanorm"):
            N, t = s["norm"], s["t"]
            if t == 0:
                N["n"] = pl.next("norms") - 1
                N["done"] = []
            if what == "metanorm":
                s["ready"] = ("s_meta", 16)
            elif what == "addnorm":
                s["ready"] = product_done[t]
            else:
                s["ready"] = (mem_ready if N["source"] == "mem" else x_ready)[t]
            s["rstd"] = pl.next("rstd")
            s["done"] = pl.next("norm_done")
            N["done"].append(s["done"])
            done = ("norm_done", s["done"])
            if what == "addnorm" or N["dest"] == "x":
                x_ready[t] = done
            elif N["dest"] == "xn":
                xn_ready[(0, t)] = xn_ready[(1, t)] = done
            else:
                other_ready[t] = done
        if what in ("turn_norm", "turn_meta", "turn_f", "turn_mix"):
            s["batch"] = pl.next("batches") - 1
            s["hi"] = pl.next("his")
            s["turned"] = pl.next("turns")
            ring(s, ("turned", s["turned"]))
            if what == "turn_norm":
                s["ready"] = xn_ready[(s["c"] // 4, s["t"])] if s["source"] == "xn" else other_ready[s["t"]]
                places = [(s["dest"], s["c"] + k, s["t"]) for k in range(4)]
            elif what == "turn_meta":
                s["ready"] = other_ready[0]
                places = [("m", s["c"] + k, t) for k in range(4) for t in range(NT)]
            elif what == "turn_f":
                places = [("m", (2 * s["j"] + c) % KC, t) for c in range(2) for t in range(NT)]
            else:
                places = [(name, c, t) for name, c in g["mix"] for t in range(NT)]
                g["mixed"] = s["batch"] + 1
            last = [reader[p]["u"] + 1 for p in places if p in reader]
            assert all("ended" in reader[p] for p in places if p in reader)
            s["dest_free"] = ("unit_used", max(last)) if last else None


def make_plan(W):
    pl = Plan()
    line = []

    def cols(w, rows, *ranges):
        return (w, rows, ranges)

    def add(gi):
        line.extend(("unit", u) for u in gi["units"])

    def units_of(loads_of, operand):
        return [((c, c + UK), loads_of(c), operand) for c in range(0, KC, UK)]

    def norm(what="norm", **kw):
        N = dict(**kw)
        return [(what, dict(norm=N, t=t)) for t in range(1 if what == "metanorm" else NT)]

    def norm_turns(source, dest, t):
        return [("turn_norm", dict(source=source, dest=dest, t=t, c=c)) for c in range(0, KC, 4)]

    def tile_by_tile(units, between=()):
        line.extend(("unit_a", u) for u in units)
        line.extend(between)
        line.extend(("unit_b", u) for u in units)

    w1 = [W["w_in"][layer] for layer in range(DEPTH)]
    pairs = 0

    def banks():
        nonlocal pairs
        pairs += 1
        return (0, 1) if pairs % 2 else (2, 3)

    def memory_norm():
        return (norm(source="mem", dest="mem_n"),
                [turn for t in range(NT) for turn in norm_turns("mem_n", "m", t)])

    def memory_keys(layer, extra):
        g = pl.group("mkv", banks(), units_of(
            lambda c: [(0, 1, W["w_mem_kv"][layer], c, 0, 0, 2 * MEMW)], "m"), layer=layer)
        side(g, extra)
        return ("turn_mk", dict(mkv=g))

    def side(gi, extra):
        for n, u in enumerate(gi["units"]):
            line.append(("unit", u))
            line.extend(extra.get(n, []))

    def head_group(layer, kind, p):
        base = {"sb": 0, "mb": 4 * SBW, "mem": 8 * SBW}[kind]
        if kind == "mem":
            def loads(c):
                return [(0, 1, w1[layer], c, base, 0, 512)]
            mix = [("mix", 6), ("mix", 7)]
        else:
            def loads(c):
                return [(0, 4, w1[layer], c, base + p * P, SBW, P)]
            mix = [("mix", {"sb": 0, "mb": 3}[kind] + p)]
        return pl.group(kind, banks(), units_of(loads, "h"), layer=layer, pair=p, mix=mix)

    def meta_group(n):
        c0 = ([QA] + [QA + KA + VA + QB + k * 512 for k in range(4)])[n]
        return pl.group("metakv", (n % 4,), units_of(lambda c: [(0, 1, W["w_in_2"], c, c0, 0, 512)],
                                                     "m"), n=n)

    for layer in range(DEPTH):
        if layer == 0:
            first = norm(source="x", dest="xn")
            line.extend([first[0], ("splits", 1)])
            line.extend(norm_turns("xn", "h", 0))
            line.append(("splits", SPLIT_AHEAD))
            mem_norm, turns = memory_norm()
            units = head_group(layer, "sb", 0)["units"]
            line.extend([("unit_a", units[0]), first[1], ("masks", None)])
            line.extend(("unit_a", u) for u in units[1:])
            line.extend(norm_turns("xn", "h", 1))
            line.extend(("unit_b", u) for u in units)
            line.append(("small", None))
            line.extend(mem_norm)
            side(head_group(layer, "sb", 1), {1: turns[:1], 2: turns[1:2], 3: turns[2:]})
            turn_keys = memory_keys(layer, {})
            side(head_group(layer, "sb", 2), {0: [turn_keys]})
        else:
            for p in range(3):
                side(head_group(layer, "sb", p),
                     {0: [turn_keys]} if p == 0 else {2: norm("metanorm", dest="meta_n")} if p == 2 else {})
        side(head_group(layer, "mem", 0), {})
        for p in range(3):
            extra = {}
            if layer == 0 and p == 0:
                mem_norm, turns = memory_norm()
                extra = {0: mem_norm}
            elif layer == 0 and p == 1:
                extra = {k: [turn] for k, turn in enumerate(turns)}
            elif layer == 1 and p == 1:
                extra = {k: [("turn_meta", dict(c=4 * k))] for k in range(2)}
            side(head_group(layer, "mb", p), extra)
        outs = [pl.group("wo", banks(), units_of(
            lambda c, n=n: [(0, 1, W["w_out"][layer], c, n * 512, 0, 512)], "mix"),
            layer=layer, n=n) for n in range(2)]
        a, b = (o["units"] for o in outs)
        for us in (a, b):
            us[2]["chunks"], us[3]["chunks"] = us[3]["chunks"], us[2]["chunks"]
            us[2]["loads"], us[3]["loads"] = us[3]["loads"], us[2]["loads"]
        line.extend(("unit", u) for u in a[:3] + b[:3])
        line.append(("flush", None))
        line.extend(("unit_a", u) for u in (a[3], b[3]))
        if layer < DEPTH - 1:
            after = norm(source="x", dest="xn")
            line.append(after[0])
            line.extend(("unit_b", u) for u in (a[3], b[3]))
            turn_keys = memory_keys(layer + 1, {0: [after[1]], 2: norm_turns("xn", "h", 0), 3: norm_turns("xn", "h", 1)})
        else:
            final, after = norm(source="x", dest="x"), norm(source="x", dest="xn")
            line.append(final[0])
            line.extend(("unit_b", u) for u in (a[3], b[3]))
            beside = {0: {0: [after[0]], 2: [final[1]], 3: [("rope_meta", dict(n=0))]},
                      1: {0: [after[1]], 3: [("rope_meta", dict(n=1))]},
                      2: {3: [("rope_meta", dict(n=2))]},
                      3: {3: norm_turns("xn", "h", 0)},
                      4: {1: norm_turns("xn", "h", 1)}}
    w2 = W["w_in_2"]
    for n in range(5):
        side(meta_group(n), beside[n])
    for kv in range(KVH):
        def loads(c, kv=kv):
            return [(0, 1, w2, c, kv * 256, 0, 256), (256, 2, w2, c, QA + kv * DH, KA, DH)]
        add(pl.group("swa", (0, 1), units_of(loads, "h"), kv=kv,
                     mix=[("mix", 2 * kv), ("mix", 2 * kv + 1)]))
    for d in range(DIFF_HEADS):
        def loads(c, d=d):
            return [(0, 3, w2, c, QA + KA + VA + d * P, QB, P)]
        add(pl.group("diff", (0, 1), units_of(loads, "h"), d=d, mix=[("m", d)]))
    for n in range(2):
        add(pl.group("bswa", (0, 1), units_of(
            lambda c, n=n: [(0, 1, W["w_branch_swa_2"], c, n * 512, 0, 512)], "mix"), n=n))
    for n in range(4):
        g = pl.group("gates", (0, 1), units_of(
            lambda c, n=n: [(0, 1, w2, c, IN2 - 2 * D + n * 512, 0, 512)], "h"), n=n)
        side(g, {2: [("flush", None), ("settle", None)]} if n == 0 else
             {1: [("gate_swa", dict(n=n - 1))]} if n < 3 else {3: [("tables", None)]})
    bd = [pl.group("bdiff", (2, 3) if n == 0 else (4, 5), units_of(
        lambda c, n=n: [(0, 1, W["w_branch_diff_2"], c, n * 512, 0, 512)], "m"), n=n)
        for n in range(2)]
    add(bd[0])
    side(bd[1], {1 + t: [norm_turns("xn", "mix", t)[0]] for t in range(NT)})
    wo2 = [pl.group("wo2", (n, 2 + n), units_of(
        lambda c, n=n: [(0, 1, W["w_out_2"], c, n * 512, 0, 512)], "mix"), n=n) for n in range(2)]
    a, b = (g["units"] for g in wo2)
    line.extend(("unit", u) for u in a[:2])
    for t in range(NT):
        line.append(norm_turns("xn", "mix", t)[1])
    line.extend(("unit", u) for u in b[:2])
    post, pre = norm("addnorm"), norm(source="x", dest="xn")
    tile_by_tile(a[2:] + b[2:], [post[0], pre[0]])
    line.extend(norm_turns("xn", "h", 0) + [post[1]])
    nf = DFF // 256
    fin = []
    for j in range(nf):
        def loads(c, j=j):
            return [(0, 2, W["w_ffn_in_2"], c, j * 256, DFF, 256)]
        fin.append((j, units_of(loads, "h")))

    fo = [pl.group("fout", (n, 2 + n), [], n=n) for n in range(2)]

    def outs_of(j):
        return [dict(loads=[(0, 1, W["w_ffn_out_2"], 2 * j, n * 512, 0, 512)],
                     operand="f", chunks=(2 * j, 2 * j + UK), g=fo[n],
                     first=(j == 0), last=(j == nf - 1)) for n in range(2)]

    for j, us in fin:
        g = pl.group("ffn", (4, 5), us, j=j)
        if j == 0:
            line.extend(("unit_a", u) for u in g["units"][:2])
            line.append(pre[1])
            line.extend(("unit_a", u) for u in g["units"][2:])
            line.extend(norm_turns("xn", "h", 1))
            line.extend(("unit_b", u) for u in g["units"])
        else:
            line.extend(("unit", u) for u in g["units"][:2])
            line.append(("turn_f", dict(j=j - 1, f=last_g)))
            line.extend(("unit", u) for u in g["units"][2:])
            if j < nf - 1:
                line.extend(("unit", u) for u in outs_of(j - 1))
        last_g = g
    line.append(("tables", None))
    held = outs_of(nf - 2)
    line.extend(("unit_a", u) for u in held)
    line.append(("turn_f", dict(j=nf - 1, f=last_g)))
    last_outs = outs_of(nf - 1)
    line.extend(("unit_a", u) for u in last_outs)
    final = norm("addnorm")
    line.append(final[0])
    line.extend(("unit_b", u) for u in held + last_outs)
    line.append(final[1])
    pl.steps = lay_out(line)
    number(pl, pl.steps)
    return pl


def build(nc, A, out):
    W = dict(w_in=[A["w_in"][i] for i in range(DEPTH)], w_mem_kv=[A["w_mem_kv"][i] for i in range(DEPTH)],
             w_out=[A["w_out"][i] for i in range(DEPTH)])
    for name in ("w_in_2", "w_branch_swa_2", "w_branch_diff_2", "w_out_2", "w_ffn_in_2", "w_ffn_out_2"):
        W[name] = A[name][0]
    pl = make_plan(W)
    U, STEPS = pl.units, pl.steps
    cf_np, cb_np = constant_tables()
    cf_dram = nc.inline_tensor(cf_np, name="const_f32").ap()
    cb_dram = nc.inline_tensor(cb_np, name="const_masks").ap()

    ctx = ExitStack()
    with ctx:
        def sb(name, shape, dt=F32):
            return ctx.enter_context(nc.sbuf_tensor(name, shape, dt))

        def sem(name):
            return ctx.enter_context(nc.semaphore(name))

        psum = ctx.enter_context(nc.psum_tensor("psum", [P, 8, 512], F32))

        cf = sb("cf", [P, C_END])
        cb = sb("cb", [P, B_END], BF16)
        raw = sb("raw", [P, NRAW, UK, 512])
        w_hi = sb("w_hi", [P, NSLOT, UK, 512], F32R)
        w_lo = sb("w_lo", [P, NSLOT, UK, 512], F32R)
        x = sb("x", [P, NT, D])
        xn = sb("xn", [P, NT, D])
        gates = sb("gates", [P, NT, 2 * D])
        S_hi = {"h": sb("h_hi", [P, KC, T], F32R), "m": sb("m_hi", [P, KC, T], F32R),
                "mix": sb("mix_hi", [P, KC, T], F32R)}
        S_lo = {"h": sb("h_lo", [P, KC, T], F32R), "m": sb("m_lo", [P, KC, T], F32R),
                "mix": sb("mix_lo", [P, KC, T], F32R)}
        S_hi["f"], S_lo["f"] = S_hi["m"], S_lo["m"]
        gain = sb("gain", [P, NGAIN, D])
        stage = sb("stage", [P, NSTAGE, NT, 512])
        mkv = sb("mkv", [P, NT, 2 * MEMW])
        km_t = sb("km_t", [P, 2, T])
        sgate = sb("sgate", [P, 2, NT, 256])
        gtmp = sb("gtmp", [P, NT, 256])
        qk = sb("qk", [P, 2, 784])
        probs = sb("probs", [P, 4, NT, 272])
        p_t = sb("p_t", [P, 2, 512])
        p_tm = sb("p_tm", [META, 2, NT * P])
        o_st = sb("o_st", [P, 2, NT, 256])
        sbt = sb("sbt", [P, 2, 384])
        rtmp = sb("rtmp", [P, 2, 5 * DH])
        stats = sb("stats", [P, 4, 8])
        rec = sb("rec", [P, 4, 4])
        nstat = sb("nstat", [P, 32])
        sinks = sb("sinks", [P, 32])
        lam_in = sb("lam_in", [P, 4, DH])
        lam = sb("lam", [P, 8])
        subln = sb("subln", [P, P])
        sil = gtmp
        eps_col = sb("eps_col", [P, 1])
        hstat = sb("hstat", [P, 32])

        gflat = gates[:].rearrange("p t d -> p (t d)")
        mem_v = gflat[:, 0:NT * D].rearrange("p (t d) -> p t d", t=NT)
        mem_n = gflat[:, NT * D:2 * NT * D].rearrange("p (t d) -> p t d", t=NT)
        meta_v = gflat[0:META, 0:D]
        meta_n = gflat[0:META, 3 * D:4 * D]
        META_VA, META_KB, META_VB, META_K2 = KA, KA + VA, KA + VA + KB, KA + VA + KB + VB
        meta_kv = gflat[0:META, 0:META_K2 + 2 * KA]
        SRC = {"x": x, "xn": xn, "mem": mem_v, "mem_n": mem_n}

        mask_in = probs[:].rearrange("p j t k -> p (j t k)")[:, 0:B_END]

        s_const = sem("s_const")
        s_ident = sem("s_ident")
        s_x = [sem(f"s_x{t}") for t in range(NT)]
        s_small = sem("s_small")
        s_mem = sem("s_mem")
        s_meta = sem("s_meta")
        w_landed = [sem(f"w_landed{i}") for i in range(NRAW)]
        s_gain_first = sem("s_gain_first")
        s_gain = [sem(f"s_gain{i}") for i in range(NGAIN)]
        hi_ready = sem("hi_ready")
        lo_ready = sem("lo_ready")
        unit_used = sem("unit_used")
        group_done = sem("group_done")
        evac_act = sem("evac_act")
        evac_dve = sem("evac_dve")
        gate_e = sem("gate_e")
        gate_done = sem("gate_done")
        roped = sem("roped")
        turned = sem("turned")
        pt_ready = sem("pt_ready")
        turned_hi = sem("turned_hi")
        tp_done = sem("tp_done")
        scores_done = sem("scores_done")
        negmax = sem("negmax")
        probs_ready = sem("probs_ready")
        sb_log = sem("sb_log")
        sb_soft = sem("sb_soft")
        sb_sum = sem("sb_sum")
        blended = sem("blended")
        out_done = sem("out_done")
        out_used = sem("out_used")
        head_rstd = sem("head_rstd")
        norm_done = sem("norm_done")
        rstd_ready = sem("rstd_ready")
        silu_ready = sem("silu_ready")
        meta_roped = max(s["roped"] for what, s in STEPS if what == "rope_meta")
        gates_ready = sem("gates_ready")
        lam_sums = sem("lam_sums")
        lam_exp = sem("lam_exp")
        eps_set = sem("eps_set")
        const_done = sem("const_done")
        dve_order = sem("dve_order")
        act_order = sem("act_order")
        pool_order = sem("pool_order")
        s_out = sem("s_out")

        SEM = dict(s_x0=s_x[0], s_x1=s_x[1], s_small=s_small, s_meta=s_meta,
                   group_done=group_done, unit_used=unit_used,
                   evac_act=evac_act, evac_dve=evac_dve, norm_done=norm_done, tp_done=tp_done,
                   out_done=out_done, blended=blended, s_mem=s_mem, turned=turned, out_used=out_used,
                   pt_ready=pt_ready)

        def wait(eng, what):
            if what is not None:
                eng.wait_ge(SEM[what[0]], what[1])

        def rows(w, c):
            return w[c * P:(c + UK) * P, :].rearrange("(k p) n -> p k n", p=P)

        gain_src = [A["norm_g"][0:1, :], A["mem_norm_g"][0:1, :], A["mem_norm_g"][1:2, :], A["norm_g"][1:2, :],
                    A["pre_mix_gain_2"], A["final_norm_g"].rearrange("(a n) -> a n", a=1), A["pre_mix_gain_2"],
                    A["b_gate_2"][:, 0:D], A["b_gate_2"][:, D:2 * D], A["post_mix_gain_2"],
                    A["pre_ffn_gain_2"], A["post_ffn_gain_2"]]
        gain_use = {}
        gk = 0
        gain_loads = []
        users = []
        for i, (what, s) in enumerate(STEPS):
            if what in ("norm", "metanorm", "addnorm") and s["t"] > 0:
                gain_use[i] = s["norm"]["gain"]
                users[s["norm"]["user"]] = i
                continue
            if what in ("norm", "metanorm", "addnorm") or (what == "evac" and s["g"]["kind"] == "gates"
                                                          and s["g"]["n"] % 2 == 0 and s["t"] == 0):
                n = len(gain_loads)
                gain_loads.append((gain_src[gk], n % NGAIN))
                gain_use[i] = (n % NGAIN, s_gain_first, 16) if n == 0 else \
                    (n % NGAIN, s_gain[n % NGAIN], 16 * (n // NGAIN + (n % NGAIN != 0)))
                users.append(i)
                gk += 1
                if what == "evac":
                    gate_gain = gain_use[i]
                else:
                    s["norm"]["gain"], s["norm"]["user"] = gain_use[i], n
            elif what == "evac" and s["g"]["kind"] == "gates":
                gain_use[i] = gate_gain
                users[-1] = i
        assert gk == len(gain_src)
        gain_freed = []
        for i in users:
            what, s = STEPS[i]
            if what == "evac":
                gain_freed.append((evac_dve, s["g"]["free"][-1]))
            else:
                gain_freed.append((norm_done, s["norm"]["done"][-1]))
        load_at = {}
        for n in range(NGAIN, len(gain_loads)):
            load_at.setdefault(users[n - NGAIN], []).append(n)

        def load_gain(eng, n):
            src, slot = gain_loads[n]
            if n >= NGAIN:
                eng.wait_ge(*gain_freed[n - NGAIN])
            eng.dma_start(gain[:, slot, :], src.partition_broadcast(P).rearrange("p a n -> p (a n)"))\
               .then_inc(s_gain[slot] if n else s_gain_first, 16)

        def bank_free(eng, g, t):
            prev = g["prev"][t]
            if prev is not None and prev[0]["by"]:
                eng.wait_ge(SEM[prev[0]["by"]], prev[0]["free"][prev[1]])

        def turn_aps(what, s):
            bank = s["bank"]
            if what == "turn_norm":
                at = s["t"] * P
                name, c, n, lo, hi, width = s["dest"], s["c"], 4, at, at + P, P
            elif what == "turn_meta":
                name, c, n, lo, hi, width = "m", s["c"], 4, 0, META, META
            elif what == "turn_f":
                name, c, n, lo, hi, width = "f", (2 * s["j"]) % KC, 2, 0, T, T
            else:
                name, c = s["g"]["mix"][0]
                n, lo, hi, width = len(s["g"]["mix"]), 0, T, T
            src = psum[:, bank, 0:n * width].rearrange("p (c w) -> p c w", c=n)
            return (S_hi[name][:, c:c + n, lo:hi], S_lo[name][:, c:c + n, lo:hi]), src

        by_ga = {g["ga"]: g for g in pl.groups if "ga" in g}
        ffn = [g for g in pl.groups if g["kind"] == "ffn"]
        ffn_turned = [s["batch"] + 1 for what, s in STEPS if what == "turn_f"]

        block = ctx.enter_context(nc.Block())

        @block.sync
        def _(sp):
            sp.dma_start(x[:, 0, :], A["x"][0, 0:P, :]).then_inc(s_x[0], 16)
            load_gain(sp, 0)
            sp.dma_start(cf[:, 0:C_TRI], cf_dram[:, 0:C_TRI]).then_inc(s_ident, 16)
            for u in U:
                if u["u"] == 2:
                    sp.dma_start(x[:, 1, :], A["x"][0, P:T, :]).then_inc(s_x[1], 16)
                elif u["u"] == NRAW:
                    sp.dma_start(cf[:, C_TRI:C_END], cf_dram[:, C_TRI:C_END]).then_inc(s_const, 16)
                    sp.dma_start(mask_in, cb_dram).then_inc(s_const, 16)
                if u["u"] >= NRAW:
                    sp.wait_ge(lo_ready, u["u"] - NRAW + 1)
                for off, reps, w, c, c0, step, width in u["loads"]:
                    dst = raw[:, u["raw"], :, off:off + reps * width]
                    if reps == 1:
                        sp.dma_start(dst, rows(w, c)[:, :, c0:c0 + width]).then_inc(w_landed[u["raw"]], 16)
                    else:
                        for k in range(UK):
                            span = w[(c + k) * P:(c + k + 1) * P, c0:c0 + width].unsqueeze(1)
                            src = bass.AP(tensor=span.tensor, offset=span.offset,
                                          ap=[list(span.ap[0]), [step, reps], [1, width]])
                            sp.dma_start(dst[:, k, :].rearrange("p (i n) -> p i n", i=reps), src)\
                              .then_inc(w_landed[u["raw"]], 16)
            for t in range(NT):
                sp.wait_ge(norm_done, STEPS[-1][1]["norm"]["done"][t])
                sp.dma_start(out[0, t * P:(t + 1) * P, :], x[:, t, :]).then_inc(s_out, 16)
            sp.wait_ge(s_out, 16 * NT)

        @block.gpsimd
        def _(pool):
            pool.wait_ge(s_x[1], 16)
            load_gain(pool, 1)
            pool.dma_start(mem_v, A["mem"][0].rearrange("(t p) d -> p t d", p=P)).then_inc(s_mem, 16)
            pool.dma_start(sinks[:, 0:16], A["attn_sink_2"].partition_broadcast(P)
                           .rearrange("p a n -> p (a n)")).then_inc(s_small, 16)
            for i, name in enumerate(("lambda_q1_2", "lambda_k1_2", "lambda_q2_2", "lambda_k2_2")):
                pool.dma_start(lam_in[:, i, :], A[name].partition_broadcast(P)
                               .rearrange("p a n -> p (a n)")).then_inc(s_small, 16)
            pool.dma_start(subln[:], A["diff_subln_gain_2"].partition_broadcast(P)
                           .rearrange("p a n -> p (a n)")).then_inc(s_small, 16)
            order = [0]

            def link(ins):
                order[0] += 1
                ins.then_inc(pool_order, 1)
                pool.wait_ge(pool_order, order[0])

            pool.wait_ge(s_const, 32)
            memory_norms = 0
            for i, (what, s) in enumerate(STEPS):
                if what == "norm" and s["norm"]["source"] == "mem" and s["t"] == NT - 1:
                    memory_norms += 1
                    if memory_norms == DEPTH:
                        pool.wait_ge(norm_done, s["done"])
                        pool.dma_start(meta_v, A["meta_tokens_2"]).then_inc(s_meta, 16)
                for n in load_at.get(i, []):
                    load_gain(pool, n)
                if what == "rope_meta":
                    pool.wait_ge(evac_act, s["ready"])
                    cm, smn = cf[0:META, C_COSM:C_COSM + DH], cf[0:META, C_SINM:C_SINM + DH]
                    half = DH // 2
                    n = s["n"]
                    for k0 in [0] if n == 0 else [META_KB + k * 4 * DH for k in (2 * n - 2, 2 * n - 1)]:
                        vm = meta_kv[:, k0:k0 + 4 * DH].rearrange("p (h d) -> p h d", d=DH)
                        am = rtmp[0:META, 0, 0:4 * DH].rearrange("p (h d) -> p h d", d=DH)
                        bm = rtmp[0:META, 1, 0:4 * DH].rearrange("p (h d) -> p h d", d=DH)
                        nc.gpsimd.tensor_tensor(am, vm, cm.unsqueeze(1).to_broadcast([META, 4, DH]), ALU.mult)
                        nc.gpsimd.tensor_tensor(bm[:, :, 0:half], vm[:, :, half:DH],
                                                smn[:, 0:half].unsqueeze(1).to_broadcast([META, 4, half]),
                                                ALU.mult)
                        link(nc.gpsimd.tensor_tensor(bm[:, :, half:DH], vm[:, :, 0:half],
                                                     smn[:, half:DH].unsqueeze(1).to_broadcast([META, 4, half]),
                                                     ALU.mult))
                        last = nc.gpsimd.tensor_tensor(vm, am, bm, ALU.add)
                        if n == 0 or k0 == META_KB + (2 * n - 2) * 4 * DH:
                            link(last)
                    if n == 0:
                        twice = meta_kv[:, META_K2:META_K2 + 2 * KA].rearrange("p (h i d) -> p h i d", i=2, d=DH)
                        once = meta_kv[:, 0:KA].rearrange("p (h d) -> p h d", d=DH)
                        nc.gpsimd.tensor_copy(twice[:, :, 0, :], once)
                        last = nc.gpsimd.tensor_copy(twice[:, :, 1, :], once)
                    last.then_inc(roped, 1)
                    pool.wait_ge(roped, s["roped"])
                if what != "rope":
                    continue
                g = s["g"]
                st = stage[:, g["ga"] % NSTAGE]
                if g["kind"] == "mb":
                    v = st[:, :, 0:256].rearrange("p t (h d) -> p t h d", d=DH)
                    nh, w, half = 4, ROPE1, ROPE1 // 2
                    cos, sin = C_COS1, C_SIN1
                else:
                    nh = 5 if g["kind"] == "swa" else 4
                    v = st[:, :, 0:nh * DH].rearrange("p t (h d) -> p t h d", d=DH)
                    w, half = DH, DH // 2
                    cos, sin = C_COS2, C_SIN2
                a = rtmp[:, 0, 0:nh * w].rearrange("p (h d) -> p h d", h=nh)
                b = rtmp[:, 1, 0:nh * w].rearrange("p (h d) -> p h d", h=nh)
                ct = cf[:, cos:cos + NT * w].rearrange("p (t d) -> p t d", t=NT)
                sn = cf[:, sin:sin + NT * w].rearrange("p (t d) -> p t d", t=NT)
                for t in range(NT):
                    pool.wait_ge(evac_act, g["free"][t])
                    shape = [P, nh, w]
                    hs = [P, nh, half]
                    nc.gpsimd.tensor_tensor(a, v[:, t, :, 0:w], ct[:, t].unsqueeze(1).to_broadcast(shape),
                                            ALU.mult)
                    nc.gpsimd.tensor_tensor(b[:, :, 0:half], v[:, t, :, half:w],
                                            sn[:, t, 0:half].unsqueeze(1).to_broadcast(hs), ALU.mult)
                    link(nc.gpsimd.tensor_tensor(b[:, :, half:w], v[:, t, :, 0:half],
                                                 sn[:, t, half:w].unsqueeze(1).to_broadcast(hs), ALU.mult))
                    last = nc.gpsimd.tensor_tensor(v[:, t, :, 0:w], a, b, ALU.add)
                    if t < NT - 1:
                        link(last)
                if g["kind"] == "swa":
                    link(last)
                    last = nc.gpsimd.tensor_copy(st[:, :, 320:384], st[:, :, 256:320])
                last.then_inc(roped, 1)
                pool.wait_ge(roped, g["roped"])

        @block.tensor
        def _(pe):
            pe.wait_ge(s_ident, 16)

            def turn(pairs):
                for o, i, n in pairs:
                    last = nc.tensor.transpose(o, i, cf[0:n, C_ID:C_ID + n])
                last.then_inc(tp_done, 1)

            where = {}
            for i, (what, s) in enumerate(STEPS):
                if what in ("unit", "unit_end"):
                    u, g = s, s["g"]
                    t = 0 if what == "unit" or g["kind"] == "metakv" else 1
                    pe.wait_ge(hi_ready, u["u"] + 1)
                    pe.wait_ge(lo_ready, u["u"] + 1)
                    name, n = u["operand"], u["width"]
                    pe.wait_ge(turned, max(where[(name, c % KC, t)] for c in range(*u["chunks"])))
                    if u["first"]:
                        bank_free(pe, g, t)
                    bank = g["banks"][t]
                    for kk in range(UK):
                        c = (u["chunks"][0] + kk) % KC
                        for z, (sx, wx) in enumerate(((S_hi, w_hi), (S_lo, w_hi), (S_hi, w_lo))):
                            last = nc.tensor.matmul(
                                psum[:, bank, 0:n], sx[name][:, c, t * P:(t + 1) * P], wx[:, u["slot"], kk, 0:n],
                                start=u["first"] and kk == 0 and z == 0, stop=u["last"] and kk == UK - 1 and z == 2,
                                skip_group_check=True)
                    if what == "unit_end":
                        last.then_inc(unit_used, 1)
                    elif u["last"]:
                        last.then_inc(group_done, 1)
                elif what in ("turn_norm", "turn_meta"):
                    b = s["batch"]
                    wait(pe, s["bank_free"])
                    wait(pe, s["ready"])
                    bank = s["bank"]
                    if what == "turn_norm":
                        src = SRC[s["source"]]
                        turn([(psum[:, bank, k * P:(k + 1) * P],
                                  src[:, s["t"], (s["c"] + k) * P:(s["c"] + k + 1) * P], P) for k in range(4)])
                        for k in range(4):
                            where[(s["dest"], s["c"] + k, s["t"])] = s["turned"]
                    else:
                        turn([(psum[:, bank, k * META:(k + 1) * META],
                                  meta_n[:, (s["c"] + k) * P:(s["c"] + k + 1) * P], META) for k in range(4)])
                        for k in range(4):
                            where[("m", s["c"] + k, 0)] = s["turned"]
                elif what == "turn_f":
                    b = s["batch"]
                    wait(pe, s["bank_free"])
                    pe.wait_ge(evac_dve, s["f"]["free"][-1])
                    bank = s["bank"]
                    turn([(psum[:, bank, (c * NT + t) * P:(c * NT + t + 1) * P],
                              o_st[:, s["j"] % 2, t, c * P:(c + 1) * P], P)
                             for c in range(2) for t in range(NT)])
                    for c in range(2):
                        for t in range(NT):
                            where[("f", (2 * s["j"] + c) % KC, t)] = s["turned"]
                elif what == "turn_qk":
                    g = s["g"]
                    K = KINDS[g["kind"]]
                    st = stage[:, g["ga"] % NSTAGE]
                    if "roped" in g:
                        pe.wait_ge(roped, g["roped"])
                    pe.wait_ge(evac_act, g["free"][-1])
                    wait(pe, s["bank_free"])
                    bank = s["bank"]
                    if s["part"] == 0:
                        tiles = [(t, K["q"] + c * P) for c in range(K["qw"] // P) for t in range(NT)]
                        if g["kind"] in ("sb", "mb"):
                            tiles += [(t, K["k"]) for t in range(NT)]
                        turn([(psum[:, bank, n * P:(n + 1) * P], st[:, t, c0:c0 + P], P)
                              for n, (t, c0) in enumerate(tiles)])
                    else:
                        pe.wait_ge(roped, meta_roped)
                        k0 = META_K2 + g["kv"] * P if g["kind"] == "swa" else META_KB + g["d"] * P
                        turn([(psum[:, bank, t * P:(t + 1) * P], st[:, t, K["k"]:K["k"] + P], P)
                              for t in range(NT)]
                             + [(psum[:, bank, T:T + META], meta_kv[:, k0:k0 + P], META)])
                elif what == "turn_mk":
                    pe.wait_ge(evac_act, s["mkv"]["free"][-1])
                    wait(pe, s["bank_free"])
                    turn([(psum[:, s["bank"], (c * NT + t) * P:(c * NT + t + 1) * P],
                           mkv[:, t, c * P:(c + 1) * P], P) for c in range(2) for t in range(NT)])
                elif what == "scores":
                    g = s["g"]
                    kind, j, a = g["kind"], s["j"], s["a"]
                    pe.wait_ge(turned, g["qk_ready"])
                    if j >= 2:
                        pe.wait_ge(probs_ready, j - 1)
                    if s["meta_out"]:
                        pe.wait_ge(pt_ready, s["meta_out"])
                    lo = 64 * (a % 2)
                    buf = qk[lo:lo + 64, g["ga"] % 2]
                    qoff = (a // 2) * T if kind in ("swa", "mem") else 0
                    koff = 2 * P * (KINDS[kind]["qw"] // P)

                    def mm(o, l, r, start, stop=True):
                        return nc.tensor.matmul(o, l, r, start=start, stop=stop, skip_group_check=True)

                    idb = cb[:, B_ID:B_ID + P]
                    if kind == "sb":
                        S = psum[:, 4 + j % 2]
                        mm(S[:, 0:T], buf[:, koff:koff + P], buf[:, 0:T], True, False)
                        mm(S[:, T:T + P], buf[:, koff + P:koff + T], buf[:, P:T], False, False)
                        mm(S[:, 0:P], idb, cb[:, B_SB:B_SB + P], False, False)
                        last = mm(S[:, T:T + P], idb, cb[:, B_SB:B_SB + P], False, True)
                    elif kind == "mb":
                        S = psum[:, 4 + j % 2]
                        mm(S[:, 0:P], buf[:, 0:P], buf[:, koff:koff + P], True, False)
                        mm(S[:, T:2 * T], buf[:, P:T], buf[:, koff:koff + T], False, False)
                        mm(S[:, 0:P], idb, cb[:, B_LOW:B_LOW + P], False, False)
                        last = mm(S[:, T + P:2 * T], idb, cb[:, B_LOW:B_LOW + P], False, True)
                    elif kind == "mem":
                        pe.wait_ge(turned, g["km_ready"])
                        S = psum[:, 4 + j % 2]
                        keys = km_t[lo:lo + 64, a // 2, :]
                        mm(S[:, 0:T], buf[:, qoff:qoff + P], keys, True, False)
                        last = mm(S[:, T:2 * T], buf[:, qoff + P:qoff + T], keys, False, True)
                    else:
                        for t in range(NT):
                            S = psum[:, 2 + 2 * (j % 2) + t]
                            q = buf[:, qoff + t * P:qoff + (t + 1) * P]
                            last = mm(S[:, 0:T + META], q, buf[:, koff:koff + T + META], True, kind == "diff")
                            if kind == "swa":
                                m = B_LOW if t == 0 else B_UP
                                at = P if t == 0 else 0
                                last = mm(S[:, at:at + P], idb, cb[:, m:m + P], False, True)
                    last.then_inc(scores_done, 1)
                elif what == "later":
                    j = s["j"]
                    pe.wait_ge(sb_soft, s["sb"] + 1)
                    S = psum[:, 4 + j % 2]
                    r = sbt[:, j % 2]
                    nc.tensor.matmul(S[:, 0:384], cf[:, C_TRI:C_TRI + P], r[:, 0:384], start=False, stop=False,
                                     skip_group_check=True)
                    nc.tensor.matmul(S[:, P:T], cf[:, C_ONE:C_ONE + P], r[:, T:384], start=False, stop=True,
                                     skip_group_check=True).then_inc(sb_sum, 1)
                elif what == "turn_p":
                    g = s["g"]
                    kind, j, b = g["kind"], s["j"], s["batch"]
                    wait(pe, s["bank_free"])
                    if kind == "diff":
                        pe.wait_ge(blended, s["blended"])
                    else:
                        pe.wait_ge(probs_ready, j + 1)
                    pr = probs[:, j % 4]
                    blocks = [(0, 0), (1, 0), (1, 1)] if kind == "mb" else [(0, 0), (0, 1), (1, 0), (1, 1)]
                    todo = [(psum[:, s["bank"], n * P:(n + 1) * P], pr[:, t, k * P:(k + 1) * P], P)
                            for n, (t, k) in enumerate(blocks)]
                    if kind in ("swa", "diff"):
                        todo += [(psum[0:META, 2 + 2 * (j % 2) + t, 384:512], pr[:, t, T:T + META], P)
                                 for t in range(NT)]
                    turn(todo)
                elif what == "out":
                    g = s["g"]
                    kind, j, o = g["kind"], s["j"], s["o"]
                    vs = stage[:, g["ga"] % NSTAGE]
                    wide = P if kind == "diff" else DH
                    if kind == "mem":
                        vs, v0 = mkv, MEMW + s["a"] * DH
                    else:
                        v0 = KINDS[kind]["v"] + (s["a"] * DH if kind in ("sb", "mb") else 0)
                    if kind == "swa":
                        vm = meta_kv[:, META_VA + g["kv"] * DH:META_VA + (g["kv"] + 1) * DH]
                    elif kind == "diff":
                        vm = meta_kv[:, META_VB + g["d"] * P:META_VB + (g["d"] + 1) * P]
                    if kind == "sb":
                        pe.wait_ge(probs_ready, j + 1)
                        src = probs[:, j % 4].rearrange("p t k -> p (t k)")
                        blocks = [[(0, 0)], [(1, 0), (2, 1)]]
                    else:
                        pe.wait_ge(pt_ready, s["pt"] + 1)
                        src = p_t[:, s["pt"] % 2]
                        blocks = [[(0, 0)], [(1, 0), (2, 1)]] if kind == "mb" \
                            else [[(0, 0), (1, 1)], [(2, 0), (3, 1)]]
                    wait(pe, s["out_bank_free"])
                    for t in range(NT):
                        dst = psum[:, s["out_bank"], t * wide:(t + 1) * wide]
                        for n, (blk, kt) in enumerate(blocks[t]):
                            end = n == len(blocks[t]) - 1 and kind not in ("swa", "diff")
                            last = nc.tensor.matmul(dst, src[:, blk * P:(blk + 1) * P], vs[:, kt, v0:v0 + wide],
                                                    start=(n == 0), stop=end)
                        if kind in ("swa", "diff"):
                            last = nc.tensor.matmul(dst, p_tm[:, s["pt"] % 2, t * P:(t + 1) * P], vm,
                                                    start=False, stop=True)
                    last.then_inc(out_done, 1)
                elif what == "turn_mix":
                    g = s["g"]
                    b = s["batch"]
                    wait(pe, s["bank_free"])
                    pe.wait_ge(out_used, g["last_out"])
                    turn([(psum[:, s["bank"], (c * NT + t) * P:(c * NT + t + 1) * P],
                              o_st[:, g["ga"] % 2, t, c * P:(c + 1) * P], P)
                             for c in range(len(g["mix"])) for t in range(NT)])
                    for name, c in g["mix"]:
                        for t in range(NT):
                            where[(name, c, t)] = s["turned"]
                elif what == "small":
                    pe.wait_ge(const_done, 1)
                elif what == "settle":
                    pe.wait_ge(probs_ready, pl.count["jobs"])

        @block.scalar
        def _(act):
            order = [0]

            def link(ins):
                order[0] += 1
                ins.then_inc(act_order, 1)
                act.wait_ge(act_order, order[0])

            def split(u):
                act.wait_ge(w_landed[u["raw"]], u["landed"])
                if u["u"] >= NSLOT:
                    act.wait_ge(unit_used, u["u"] - NSLOT + 1)
                n = u["width"]
                nc.scalar.activation(w_hi[:, u["slot"], :, 0:n], raw[:, u["raw"], :, 0:n], ACT.Copy)\
                    .then_inc(hi_ready, 1)

            nc.scalar.preload_act_table_set("natural_log_exp_and_others")
            act.wait_ge(eps_set, 1)
            for i, (what, s) in enumerate(STEPS):
                if what == "split":
                    split(s)
                elif what in ("norm", "addnorm", "metanorm"):
                    N, t = s["norm"], s["t"]
                    wait(act, s["ready"])
                    if what == "norm":
                        srct = SRC[N["source"]][:, t, :]
                        junk = (xn if N["source"] != "mem" else mem_n)[:, t, :]
                    elif what == "metanorm":
                        srct, junk = meta_v, meta_n
                    else:
                        srct, junk = psum[:, 2 * t:2 * t + 2, :].rearrange("p b n -> p (b n)"), xn[:, t, :]
                    rowsn = META if what == "metanorm" else P
                    c = 4 * (N["n"] % 4) + 2 * t
                    ss = nstat[0:rowsn, c:c + 1]
                    rs = nstat[0:rowsn, 16 + c:17 + c]
                    link(nc.scalar.activation(junk, srct, ACT.Square, accum_out=ss))
                    link(nc.scalar.activation(ss, ss, ACT.Ln, scale=1.0 / D, bias=eps_col[0:rowsn, :]))
                    nc.scalar.activation(rs, ss, ACT.Exp, scale=-0.5).then_inc(rstd_ready, 1)
                elif what in ("turn_norm", "turn_meta", "turn_f", "turn_mix"):
                    b = s["batch"]
                    act.wait_ge(tp_done, b + 1)
                    wait(act, s["dest_free"])
                    dst, src = turn_aps(what, s)
                    nc.scalar.activation(dst[0], src, ACT.Copy).then_inc(turned_hi, 1)
                elif what == "evac":
                    g, t = s["g"], s["t"]
                    kind = g["kind"]
                    ps = psum[:, g["banks"][t]]
                    if kind != "gates":
                        wait(act, g["t_done"][t])
                    if kind in KINDS:
                        K = KINDS[kind]
                        st = stage[:, g["ga"] % NSTAGE]
                        if g["ga"] >= NSTAGE and t == 0:
                            act.wait_ge(out_done, by_ga[g["ga"] - NSTAGE]["last_out"])
                        nc.scalar.activation(st[:, t, 0:K["qw"]], ps[:, 0:K["qw"]], ACT.Copy, scale=SCALE)
                        if kind == "swa":
                            last = nc.scalar.activation(
                                st[:, t, 256:512].rearrange("p (i n) -> p i n", i=2)[:, :, 0:DH],
                                ps[:, 256:384].rearrange("p (i n) -> p i n", i=2), ACT.Copy)
                        else:
                            last = nc.scalar.activation(st[:, t, K["qw"]:K["n"]], ps[:, K["qw"]:K["n"]], ACT.Copy)
                        last.then_inc(evac_act, 1)
                    elif kind == "mkv":
                        if s["mem_before"]:
                            act.wait_ge(out_done, s["mem_before"]["last_out"])
                        nc.scalar.activation(mkv[:, t, :], ps, ACT.Copy).then_inc(evac_act, 1)
                    elif kind == "metakv":
                        nc.scalar.activation(meta_kv[:, g["n"] * 512:(g["n"] + 1) * 512], ps[0:META, :], ACT.Copy)\
                            .then_inc(evac_act, 1)
                    elif kind == "ffn":
                        if g["j"] >= 1:
                            act.wait_ge(evac_dve, ffn[g["j"] - 1]["free"][t])
                        nc.scalar.activation(sil[:, t, :], ps[:, 0:256], ACT.Silu).then_inc(silu_ready, 1)
                    elif kind == "gates":
                        act.wait_ge(evac_dve, g["free"][t])
                        gt = gates[:, t, g["n"] * 512:(g["n"] + 1) * 512]
                        nc.scalar.activation(gt, gt, ACT.Sigmoid).then_inc(gates_ready, 1)
                elif what == "tables":
                    nc.scalar.preload_act_table_set("natural_log_exp_and_others")
                elif what == "small":
                    act.wait_ge(lam_sums, 1)
                    nc.scalar.activation(lam[:, 2:4], lam[:, 0:2], ACT.Exp).then_inc(lam_exp, 1)
                elif what == "gate":
                    g, t = s["g"], s["t"]
                    c0, gw = KINDS[g["kind"]]["g"], KINDS[g["kind"]]["qw"]
                    act.wait_ge(evac_act, g["free"][t])
                    if s["before"]:
                        act.wait_ge(gate_done, s["before"])
                    nc.scalar.activation(gtmp[:, t, 0:gw], stage[:, g["ga"] % NSTAGE, t, c0:c0 + gw], ACT.Exp,
                                         scale=-1.0).then_inc(gate_e, 1)
                elif what == "scores":
                    g = s["g"]
                    kind, j = g["kind"], s["j"]
                    wait(act, s["p_free"])
                    if kind == "sb":
                        S = psum[:, 4 + j % 2, 0:384]
                        pr = probs[:, j % 4].rearrange("p t k -> p (t k)")[:, 0:384]
                        act.wait_ge(scores_done, j + 1)
                        link(nc.scalar.activation(pr, S, ACT.Abs))
                        link(nc.scalar.activation(pr, pr, ACT.Exp, scale=-1.0))
                        nc.scalar.activation(pr, pr, ACT.Ln, bias=1.0).then_inc(sb_log, 1)
                    else:
                        act.wait_ge(negmax, s["soft"] + 1)
                        stt = stats[:, j % 4]
                        for t in range(NT):
                            if kind in ("mb", "mem"):
                                n = P if (kind == "mb" and t == 0) else T
                                src = psum[:, 4 + j % 2, t * T:t * T + n]
                            else:
                                n = T + META
                                src = psum[:, 2 + 2 * (j % 2) + t, 0:n]
                            last = nc.scalar.activation(probs[:, j % 4, t, 0:n], src, ACT.Exp,
                                                        bias=stt[:, t:t + 1], accum_out=stt[:, 2 + t:3 + t])
                        if kind == "swa":
                            last = nc.scalar.activation(stt[:, 6:8], stt[:, 4:6], ACT.Exp)
                        last.then_inc(probs_ready, 1)
                elif what == "later":
                    j = s["j"]
                    act.wait_ge(sb_sum, s["sb"] + 1)
                    pr = probs[:, j % 4].rearrange("p t k -> p (t k)")[:, 0:384]
                    nc.scalar.activation(pr, psum[:, 4 + j % 2, 0:384], ACT.Exp).then_inc(probs_ready, 1)
                elif what == "turn_p":
                    kind = s["g"]["kind"]
                    act.wait_ge(tp_done, s["batch"] + 1)
                    if s["pt"] >= 2:
                        act.wait_ge(out_done, s["pt_free"])
                    n = 384 if kind == "mb" else 512
                    last = nc.scalar.activation(p_t[:, s["pt"] % 2, 0:n], psum[:, s["bank"], 0:n], ACT.Copy)
                    if kind in ("swa", "diff"):
                        b0 = 2 + 2 * (s["j"] % 2)
                        last = nc.scalar.activation(p_tm[:, s["pt"] % 2, :].rearrange("p (t q) -> p t q", t=NT),
                                                    psum[0:META, b0:b0 + 2, 384:512], ACT.Copy)
                    last.then_inc(pt_ready, 1)
                elif what == "out" and s["g"]["kind"] == "diff":
                    act.wait_ge(out_done, s["o"] + 1)
                    d = s["g"]["d"]
                    c = 4 * (d % 4)
                    for t in range(NT):
                        last = nc.scalar.activation(sil[:, t, 0:P], psum[:, s["out_bank"], t * P:(t + 1) * P], ACT.Square,
                                                    accum_out=hstat[:, c + t:c + t + 1])
                    link(last)
                    link(nc.scalar.activation(hstat[:, c + 2:c + 4], hstat[:, c:c + 2], ACT.Ln, scale=1.0 / P,
                                              bias=eps_col[:, :]))
                    nc.scalar.activation(hstat[:, 16 + c:18 + c], hstat[:, c + 2:c + 4], ACT.Exp, scale=-0.5)\
                        .then_inc(head_rstd, 1)

        @block.vector
        def _(dve):
            order = [0]

            def link(ins):
                order[0] += 1
                ins.then_inc(dve_order, 1)
                dve.wait_ge(dve_order, order[0])

            def split(u):
                dve.wait_ge(w_landed[u["raw"]], u["landed"])
                dve.wait_ge(hi_ready, u["u"] + 1)
                if u["u"] >= NSLOT:
                    dve.wait_ge(unit_used, u["u"] - NSLOT + 1)
                n = u["width"]
                nc.vector.tensor_tensor(w_lo[:, u["slot"], :, 0:n], raw[:, u["raw"], :, 0:n],
                                        w_hi[:, u["slot"], :, 0:n].bitcast(F32), ALU.subtract)\
                    .then_inc(lo_ready, 1)

            nc.vector.memset(eps_col[:], EPS).then_inc(eps_set, 1)
            for i, (what, s) in enumerate(STEPS):
                if what == "split":
                    split(s)
                elif what == "masks":
                    dve.wait_ge(s_const, 32)
                    nc.vector.tensor_copy(cb[:], mask_in).then_inc(const_done, 1)
                elif what == "small":
                    dve.wait_ge(s_small, 16 * SMALL)
                    for i in range(2):
                        link(nc.vector.tensor_tensor(lam_in[:, 2 * i, :], lam_in[:, 2 * i, :], lam_in[:, 2 * i + 1, :],
                                                     ALU.mult))
                    nc.vector.tensor_reduce(lam[:, 0:1], lam_in[:, 0, :], AX.X, ALU.add)
                    nc.vector.tensor_reduce(lam[:, 1:2], lam_in[:, 2, :], AX.X, ALU.add).then_inc(lam_sums, 1)
                    nc.vector.tensor_scalar(sinks[:, 16:32], sinks[:, 0:16], -1.0, None, ALU.mult)
                    link(nc.vector.tensor_scalar(subln[:], subln[:], 1.0 - LAMBDA_INIT, None, ALU.mult))
                    dve.wait_ge(lam_exp, 1)
                    link(nc.vector.tensor_tensor(lam[:, 4:5], lam[:, 2:3], lam[:, 3:4], ALU.subtract))
                    link(nc.vector.tensor_scalar(lam[:, 5:6], lam[:, 4:5], LAMBDA_INIT, None, ALU.add))
                elif what in ("norm", "addnorm", "metanorm"):
                    N, t = s["norm"], s["t"]
                    rowsn = META if what == "metanorm" else P
                    dve.wait_ge(*gain_use[i][1:])
                    gn = gain[0:rowsn, gain_use[i][0], :]
                    dve.wait_ge(rstd_ready, s["rstd"])
                    c = 4 * (N["n"] % 4) + 2 * t
                    rs = nstat[0:rowsn, 16 + c:17 + c]
                    if what == "norm":
                        srct, dst = SRC[N["source"]][:, t, :], SRC[N["dest"]][:, t, :]
                    elif what == "metanorm":
                        srct, dst = meta_v, meta_n
                    else:
                        srct, dst = psum[:, 2 * t:2 * t + 2, :].rearrange("p b n -> p (b n)"), xn[:, t, :]
                    last = nc.vector.scalar_tensor_tensor(out=dst, in0=srct, scalar=rs, in1=gn,
                                                          op0=ALU.mult, op1=ALU.mult)
                    if what == "addnorm":
                        link(last)
                        last = nc.vector.tensor_tensor(x[:, t, :], x[:, t, :], xn[:, t, :], ALU.add)
                    last.then_inc(norm_done, 1)
                elif what in ("turn_norm", "turn_meta", "turn_f", "turn_mix"):
                    b = s["batch"]
                    dve.wait_ge(turned_hi, s["hi"])
                    dst, src = turn_aps(what, s)
                    nc.vector.tensor_tensor(dst[1], src, dst[0].bitcast(F32), ALU.subtract).then_inc(turned, 1)
                elif what == "turn_qk":
                    g = s["g"]
                    if g["ga"] >= 2:
                        dve.wait_ge(scores_done, by_ga[g["ga"] - 2]["last_scores"])
                    q_n = NT * P * (KINDS[g["kind"]]["qw"] // P)
                    two = g["kind"] in ("swa", "diff", "mem")
                    dve.wait_ge(tp_done, s["batch"] + 1)
                    n0 = q_n if two else q_n + T
                    if s["part"] == 0:
                        nc.vector.tensor_copy(qk[:, g["ga"] % 2, 0:n0], psum[:, s["bank"], 0:n0]).then_inc(turned, 1)
                    else:
                        nc.vector.tensor_copy(qk[:, g["ga"] % 2, q_n:q_n + T + META],
                                              psum[:, s["bank"], 0:T + META]).then_inc(turned, 1)
                elif what == "turn_mk":
                    if s["mem_before"]:
                        dve.wait_ge(scores_done, s["mem_before"]["last_scores"])
                    dve.wait_ge(tp_done, s["batch"] + 1)
                    nc.vector.tensor_copy(km_t[:].rearrange("p c k -> p (c k)"), psum[:, s["bank"], :])\
                        .then_inc(turned, 1)
                elif what == "gate":
                    g, t = s["g"], s["t"]
                    c0, gw = KINDS[g["kind"]]["g"], KINDS[g["kind"]]["qw"]
                    dve.wait_ge(gate_e, s["n"] + 1)
                    gt = gtmp[:, t, 0:gw]
                    link(nc.vector.tensor_scalar(gt, gt, 1.0, None, ALU.add))
                    link(nc.vector.reciprocal(gt, gt))
                    nc.vector.tensor_tensor(sgate[:, g["ga"] % 2, t, 0:gw], gt,
                                            stage[:, g["ga"] % NSTAGE, t, c0:c0 + gw],
                                            ALU.mult).then_inc(gate_done, 1)
                    dve.wait_ge(gate_done, s["n"] + 1)
                elif what == "scores":
                    g = s["g"]
                    kind, j = g["kind"], s["j"]
                    stt = stats[:, j % 4]
                    if kind == "sb":
                        dve.wait_ge(sb_log, s["sb"] + 1)
                        if s["sb"] >= 2:
                            dve.wait_ge(sb_sum, s["sb"] - 1)
                        nc.vector.scalar_tensor_tensor(
                            out=sbt[:, j % 2], in0=psum[:, 4 + j % 2, 0:384], scalar=0.0,
                            in1=probs[:, j % 4].rearrange("p t k -> p (t k)")[:, 0:384],
                            op0=ALU.max, op1=ALU.add).then_inc(sb_soft, 1)
                        continue
                    dve.wait_ge(scores_done, j + 1)
                    if j >= 4:
                        dve.wait_ge(probs_ready, j - 3)
                    if kind == "mb":
                        nc.vector.tensor_reduce(stt[:, 0:1], psum[:, 4 + j % 2, 0:P], AX.X, ALU.max, negate=True)
                        last = nc.vector.tensor_reduce(stt[:, 1:2], psum[:, 4 + j % 2, T:2 * T], AX.X, ALU.max,
                                                       negate=True)
                    elif kind == "mem":
                        last = nc.vector.tensor_reduce(
                            stt[:, 0:2], psum[:, 4 + j % 2].rearrange("p (t k) -> p t k", t=NT), AX.X, ALU.max,
                            negate=True)
                    else:
                        b0 = 2 + 2 * (j % 2)
                        last = nc.vector.tensor_reduce(stt[:, 0:2], psum[:, b0:b0 + 2, 0:T + META], AX.X, ALU.max,
                                                       negate=True)
                        if kind == "swa":
                            hd = g["kv"] * 4 + s["a"]
                            link(last)
                            link(nc.vector.tensor_scalar(stt[:, 0:2], stt[:, 0:2], sinks[:, 16 + hd:17 + hd], None,
                                                         ALU.min))
                            last = nc.vector.tensor_scalar(stt[:, 4:6], stt[:, 0:2], sinks[:, hd:hd + 1], None,
                                                           ALU.add)
                    last.then_inc(negmax, 1)
                elif what == "blend":
                    j0 = s["j"]
                    j1 = j0 + 1
                    dve.wait_ge(probs_ready, j1 + 1)
                    nc.vector.reciprocal(rec[:, j0 % 4, 0:2], stats[:, j0 % 4, 2:4])
                    link(nc.vector.reciprocal(rec[:, j1 % 4, 0:2], stats[:, j1 % 4, 2:4]))
                    link(nc.vector.tensor_scalar(rec[:, j1 % 4, 0:2], rec[:, j1 % 4, 0:2], lam[:, 5:6], None, ALU.mult))
                    nc.vector.tensor_scalar(probs[:, j1 % 4, 0, :], probs[:, j1 % 4, 0, :], rec[:, j1 % 4, 0:1],
                                            None, ALU.mult)
                    link(nc.vector.tensor_scalar(probs[:, j1 % 4, 1, :], probs[:, j1 % 4, 1, :], rec[:, j1 % 4, 1:2],
                                                 None, ALU.mult))
                    for t in range(NT):
                        last = nc.vector.scalar_tensor_tensor(
                            out=probs[:, j0 % 4, t, :], in0=probs[:, j0 % 4, t, :], scalar=rec[:, j0 % 4, t:t + 1],
                            in1=probs[:, j1 % 4, t, :], op0=ALU.mult, op1=ALU.subtract)
                    last.then_inc(blended, 1)
                elif what == "out":
                    g = s["g"]
                    kind, j, o, a = g["kind"], s["j"], s["o"], s["a"]
                    st = o_st[:, g["ga"] % 2]
                    if s["first_out"] and g["ga"] >= 2:
                        dve.wait_ge(tp_done, by_ga[g["ga"] - 2]["mixed"])
                    if kind in ("mb", "mem", "swa"):
                        dve.wait_ge(probs_ready, j + 1)
                        if kind == "swa":
                            link(nc.vector.tensor_tensor(stats[:, j % 4, 2:4], stats[:, j % 4, 2:4],
                                                         stats[:, j % 4, 6:8], ALU.add))
                        link(nc.vector.reciprocal(rec[:, j % 4, 0:2], stats[:, j % 4, 2:4]))
                    dve.wait_ge(out_done, o + 1)
                    if kind == "sb":
                        last = nc.vector.tensor_tensor(
                            st[:, :, a * DH:(a + 1) * DH],
                            psum[:, s["out_bank"], 0:NT * DH].rearrange("p (t d) -> p t d", t=NT),
                            sgate[:, g["ga"] % 2, :, a * DH:(a + 1) * DH], ALU.mult)
                    elif kind in ("mb", "mem"):
                        for t in range(NT):
                            last = nc.vector.scalar_tensor_tensor(
                                out=st[:, t, a * DH:(a + 1) * DH], in0=psum[:, s["out_bank"], t * DH:(t + 1) * DH],
                                scalar=rec[:, j % 4, t:t + 1], in1=sgate[:, g["ga"] % 2, t, a * DH:(a + 1) * DH],
                                op0=ALU.mult, op1=ALU.mult)
                    elif kind == "swa":
                        for t in range(NT):
                            last = nc.vector.tensor_scalar(st[:, t, a * DH:(a + 1) * DH],
                                                           psum[:, s["out_bank"], t * DH:(t + 1) * DH],
                                                           rec[:, j % 4, t:t + 1], None, ALU.mult)
                    else:
                        d = g["d"]
                        c = 4 * (d % 4)
                        dve.wait_ge(head_rstd, d + 1)
                        for t in range(NT):
                            last = nc.vector.scalar_tensor_tensor(
                                out=st[:, t, 0:P], in0=psum[:, s["out_bank"], t * P:(t + 1) * P],
                                scalar=hstat[:, 16 + c + t:17 + c + t], in1=subln[:], op0=ALU.mult, op1=ALU.mult)
                    last.then_inc(out_used, 1)
                elif what == "evac":
                    g, t = s["g"], s["t"]
                    kind = g["kind"]
                    if g["by"] == "evac_act":
                        continue
                    ps = psum[:, g["banks"][t]]
                    if kind == "gates":
                        dve.wait_ge(*gain_use[i][1:])
                        dve.wait_ge(out_done, pl.count["outs"])
                    wait(dve, g["t_done"][t])
                    if kind == "wo":
                        xs = x[:, t, g["n"] * 512:(g["n"] + 1) * 512]
                        last = nc.vector.tensor_tensor(xs, xs, ps, ALU.add)
                    elif kind == "gates":
                        n = g["n"]
                        last = nc.vector.tensor_tensor(gates[:, t, n * 512:(n + 1) * 512], ps,
                                                       gain[:, gain_use[i][0], (n % 2) * 512:(n % 2) * 512 + 512],
                                                       ALU.add)
                    elif kind == "bswa":
                        last = nc.vector.tensor_copy(xn[:, t, g["n"] * 512:(g["n"] + 1) * 512], ps)
                    elif kind == "bdiff":
                        n = g["n"]
                        dve.wait_ge(gates_ready, NT * 4)
                        gt = gates[:, t, D + n * 512:D + (n + 1) * 512]
                        link(nc.vector.tensor_tensor(gt, ps, gt, ALU.mult))
                        xs = xn[:, t, n * 512:(n + 1) * 512]
                        last = nc.vector.tensor_tensor(xs, xs, gt, ALU.add)
                    elif kind == "ffn":
                        dve.wait_ge(silu_ready, g["silu"][t])
                        if g["j"] >= 2:
                            dve.wait_ge(tp_done, ffn_turned[g["j"] - 2])
                        last = nc.vector.tensor_tensor(o_st[:, g["j"] % 2, t, :], ps[:, 256:512], sil[:, t, :],
                                                       ALU.mult)
                    last.then_inc(evac_dve, 1)
                elif what == "gate_swa":
                    dve.wait_ge(gates_ready, NT * (s["n"] + 1))
                    for t in range(NT):
                        xs = xn[:, t, s["n"] * 512:(s["n"] + 1) * 512]
                        link(nc.vector.tensor_tensor(xs, xs, gates[:, t, s["n"] * 512:(s["n"] + 1) * 512],
                                                     ALU.mult))


_INS = ["x", "mem", "norm_g", "w_in", "mem_norm_g", "w_mem_kv", "w_out", "final_norm_g", "meta_tokens_2",
        "pre_mix_gain_2", "w_in_2", "b_gate_2", "attn_sink_2", "lambda_q1_2", "lambda_k1_2", "lambda_q2_2",
        "lambda_k2_2", "diff_subln_gain_2", "w_branch_swa_2", "w_branch_diff_2", "w_out_2", "post_mix_gain_2",
        "pre_ffn_gain_2", "w_ffn_in_2", "w_ffn_out_2", "post_ffn_gain_2"]


def kernel(**inputs):
    import numpy as _np
    import concourse.bacc as _bacc
    from concourse import mybir as _mybir
    from concourse.bass_utils import run_bass_kernel_spmd as _run

    nc = _bacc.Bacc("TRN2", target_bir_lowering=False, num_devices=1)
    arrays, args = {}, {}
    for name in _INS:
        a = _np.ascontiguousarray(inputs[name])
        arrays[f"in_{name}"] = a
        args[name] = nc.dram_tensor(f"in_{name}", a.shape, _mybir.dt.from_np(a.dtype), kind="ExternalInput").ap()
    out = nc.dram_tensor("out", (1, T, D), F32, kind="ExternalOutput").ap()
    build(nc, args, out)
    r = _run(nc, [arrays], core_ids=[0])
    return r.results[0]["out"]
```
